# Optimizing a Trainium2 kernel written in Bass

```python
import math
import jax, jax.numpy as jnp
from jax import lax
import numpy as np

D_MODEL = 1024
BATCH = 1
SEQ = 256
DEPTH = 2

CHUNK = 64
N_MIXERS = 3
EPS = 1e-6

SSD_EXPAND = 2
SSD_D_INNER = SSD_EXPAND * D_MODEL
SSD_HEAD_DIM = 64
SSD_HEADS = SSD_D_INNER // SSD_HEAD_DIM
SSD_GROUPS = 4
SSD_STATE = 128
SSD_CONV = 4
SSD_CONV_DIM = SSD_D_INNER + 2 * SSD_GROUPS * SSD_STATE
SSD_IN_DIM = SSD_D_INNER + SSD_CONV_DIM + SSD_HEADS

MLA_HEADS = 8
MLA_NOPE = 128
MLA_ROPE = 64
MLA_V = 128
MLA_QK = MLA_NOPE + MLA_ROPE
MLA_Q_RANK = 256
MLA_KV_RANK = 256
MLA_IN_DIM = MLA_Q_RANK + MLA_KV_RANK + MLA_ROPE
Q_BLOCK = 128
ROPE_BASE = 10000.0

RET_HEADS = D_MODEL // 256
RET_QK = 256
RET_V = 512
RET_IN_DIM = 2 * RET_HEADS * RET_QK + 2 * RET_HEADS * RET_V

FFN_DIM = 2816
N_EXPERTS = 8
TOP_K = 2
EXPERT_DIM = 3584
MOE_BLOCK = 256

N_SSD = len(range(0, DEPTH, N_MIXERS))
N_MLA = len(range(1, DEPTH, N_MIXERS))
N_RET = len(range(2, DEPTH, N_MIXERS))
N_DENSE = (DEPTH + 1) // 2
N_MOE = DEPTH // 2

kernel_name = "hybrid_ssd_mla_retention_moe_adaln"

def rms_norm(x, g):
    xf = x.astype(jnp.float32)
    y = xf * lax.rsqrt(jnp.mean(xf * xf, axis=-1, keepdims=True) + EPS)
    return (y * g.astype(jnp.float32)).astype(x.dtype)

def rotary(x, positions):
    dr = x.shape[-1]
    inv = ROPE_BASE ** (-jnp.arange(0, dr, 2, dtype=jnp.float32) / dr)
    ang = positions.astype(jnp.float32)[..., None] * inv
    cos = jnp.cos(ang)[:, :, None, :]
    sin = jnp.sin(ang)[:, :, None, :]
    xf = x.astype(jnp.float32)
    x1, x2 = xf[..., : dr // 2], xf[..., dr // 2:]
    return jnp.concatenate([x1 * cos - x2 * sin, x1 * sin + x2 * cos], axis=-1).astype(x.dtype)

def causal_dwconv(u, w, b):
    k = w.shape[0]
    out = lax.conv_general_dilated(
        u, w[:, None, :].astype(u.dtype), window_strides=(1,), padding=[(k - 1, 0)],
        dimension_numbers=("NWC", "WIO", "NWC"), feature_group_count=u.shape[-1])
    return out + b

def ssd_mixer(h, w_in, conv_w, conv_b, dt_bias, a_log, d_skip, norm_g, w_out):
    f32 = jnp.float32
    bsz, s, _ = h.shape
    nc = s // CHUNK
    G, R, P, N = SSD_GROUPS, SSD_HEADS // SSD_GROUPS, SSD_HEAD_DIM, SSD_STATE
    zxbcdt = h @ w_in
    z, xbc, dt = jnp.split(zxbcdt, [SSD_D_INNER, SSD_D_INNER + SSD_CONV_DIM], axis=-1)
    xbc = jax.nn.silu(causal_dwconv(xbc, conv_w, conv_b))
    xs, bm, cm = jnp.split(xbc, [SSD_D_INNER, SSD_D_INNER + G * N], axis=-1)
    dt = jax.nn.softplus(dt.astype(f32) + dt_bias.astype(f32))
    a_head = -jnp.exp(a_log.astype(f32)).reshape(G, R)
    xs = xs.astype(f32).reshape(bsz, nc, CHUNK, G, R, P)
    dtc = dt.reshape(bsz, nc, CHUNK, G, R)
    bm = bm.astype(f32).reshape(bsz, nc, CHUNK, G, N)
    cm = cm.astype(f32).reshape(bsz, nc, CHUNK, G, N)
    a_cum = jnp.cumsum(dtc * a_head, axis=2)
    xdt = xs * dtc[..., None]
    idx = jnp.arange(CHUNK)
    tril = (idx[:, None] >= idx[None, :])[None, None, :, :, None, None]
    seg = a_cum[:, :, :, None] - a_cum[:, :, None, :]
    decay = jnp.exp(jnp.where(tril, seg, -jnp.inf))
    cb = jnp.einsum("bclgn,bcsgn->bclsg", cm, bm)
    y_diag = jnp.einsum("bclsgr,bcsgrp->bclgrp", cb[..., None] * decay, xdt)

    def step(state, inp):
        a_c, x_c, b_c, c_c = inp
        y_off = jnp.einsum("blgn,bgrpn->blgrp", c_c, state) * jnp.exp(a_c)[..., None]
        to_end = jnp.exp(a_c[:, -1:] - a_c)
        new = state * jnp.exp(a_c[:, -1])[..., None, None] + jnp.einsum(
            "blgn,blgrp->bgrpn", b_c, x_c * to_end[..., None])
        return new, y_off

    init = jnp.zeros((bsz, G, R, P, N), f32)
    _, y_off = lax.scan(step, init, (jnp.moveaxis(a_cum, 1, 0), jnp.moveaxis(xdt, 1, 0),
                                     jnp.moveaxis(bm, 1, 0), jnp.moveaxis(cm, 1, 0)))
    y = y_diag + jnp.moveaxis(y_off, 0, 1) + xs * d_skip.astype(f32).reshape(G, R)[:, :, None]
    y = y.reshape(bsz, s, SSD_D_INNER)
    yg = (y * jax.nn.silu(z.astype(f32))).reshape(bsz, s, G, SSD_D_INNER // G)
    yg = yg * lax.rsqrt(jnp.mean(yg * yg, axis=-1, keepdims=True) + EPS)
    y = yg.reshape(bsz, s, SSD_D_INNER) * norm_g.astype(f32)
    return y.astype(h.dtype) @ w_out

def mla_mixer(h, positions, w_in, q_norm_g, kv_norm_g, w_uq, w_ukv,
              q_nope_g, q_rope_g, k_nope_g, k_rope_g, w_out):
    f32 = jnp.float32
    bsz, s, _ = h.shape
    H = MLA_HEADS
    lat = h @ w_in
    cq, ckv, k_pe = jnp.split(lat, [MLA_Q_RANK, MLA_Q_RANK + MLA_KV_RANK], axis=-1)
    q = (rms_norm(cq, q_norm_g) @ w_uq).reshape(bsz, s, H, MLA_QK)
    kv = (rms_norm(ckv, kv_norm_g) @ w_ukv).reshape(bsz, s, H, MLA_NOPE + MLA_V)
    k_nope, v = jnp.split(kv, [MLA_NOPE], axis=-1)
    q_nope, q_pe = jnp.split(q, [MLA_NOPE], axis=-1)
    q_nope = rms_norm(q_nope, q_nope_g)
    q_pe = rotary(rms_norm(q_pe, q_rope_g), positions)
    k_nope = rms_norm(k_nope, k_nope_g)
    k_pe = rotary(rms_norm(k_pe, k_rope_g)[:, :, None, :], positions)
    q = jnp.concatenate([q_nope, q_pe], axis=-1)
    k = jnp.concatenate([k_nope, jnp.broadcast_to(k_pe, (bsz, s, H, MLA_ROPE))], axis=-1)
    scale = MLA_QK ** -0.5
    nb = s // Q_BLOCK
    qb = jnp.moveaxis(q.reshape(bsz, nb, Q_BLOCK, H, MLA_QK), 1, 0)
    key_chunk = jnp.arange(s) // CHUNK

    def attend(args):
        q_blk, blk = args
        q_chunk = (blk * Q_BLOCK + jnp.arange(Q_BLOCK)) // CHUNK
        sc = jnp.einsum("bqhd,bkhd->bhqk", q_blk, k).astype(f32) * scale
        mask = key_chunk[None, :] <= q_chunk[:, None]
        p = jax.nn.softmax(jnp.where(mask, sc, -jnp.inf), axis=-1).astype(v.dtype)
        return jnp.einsum("bhqk,bkhd->bqhd", p, v)

    o = lax.map(attend, (qb, jnp.arange(nb)))
    o = jnp.moveaxis(o, 0, 1).reshape(bsz, s, H * MLA_V)
    return o @ w_out

def retention_mixer(h, positions, w_in, norm_g, w_out):
    f32 = jnp.float32
    bsz, s, _ = h.shape
    H, dk, dv = RET_HEADS, RET_QK, RET_V
    nc = s // CHUNK
    proj = h @ w_in
    q, k, v, g = jnp.split(proj, [H * dk, 2 * H * dk, 2 * H * dk + H * dv], axis=-1)
    q = rotary(q.reshape(bsz, s, H, dk), positions).astype(f32)
    k = rotary(k.reshape(bsz, s, H, dk), positions).astype(f32) * (dk ** -0.5)
    v = v.reshape(bsz, s, H, dv).astype(f32)
    log_gamma = jnp.log1p(-jnp.exp2(-5.0 - jnp.arange(H, dtype=f32)))
    idx = jnp.arange(CHUNK, dtype=f32)
    qc = q.reshape(bsz, nc, CHUNK, H, dk)
    kc = k.reshape(bsz, nc, CHUNK, H, dk)
    vc = v.reshape(bsz, nc, CHUNK, H, dv)
    d_intra = jnp.exp(log_gamma[:, None, None] * jnp.abs(idx[:, None] - idx[None, :]))
    sc = jnp.einsum("bclhd,bcshd->bchls", qc, kc) * d_intra
    y_intra = jnp.einsum("bchls,bcshe->bclhe", sc, vc)
    q_decay = jnp.exp(log_gamma[None, :] * (idx[:, None] + 1.0))
    k_decay = jnp.exp(log_gamma[None, :] * (CHUNK - 1.0 - idx[:, None]))
    chunk_decay = jnp.exp(log_gamma * CHUNK)

    def step(state, inp):
        q_c, k_c, v_c = inp
        y = jnp.einsum("blhd,bhde->blhe", q_c * q_decay[:, :, None], state)
        new = state * chunk_decay[:, None, None] + jnp.einsum(
            "blhd,blhe->bhde", k_c * k_decay[:, :, None], v_c)
        return new, y

    init = jnp.zeros((bsz, H, dk, dv), f32)
    _, y_inter = lax.scan(step, init, (jnp.moveaxis(qc, 1, 0), jnp.moveaxis(kc, 1, 0),
                                       jnp.moveaxis(vc, 1, 0)))
    y = (y_intra + jnp.moveaxis(y_inter, 0, 1)).reshape(bsz, s, H, dv)
    y = rms_norm(y, norm_g.reshape(H, dv)).reshape(bsz, s, H * dv)
    y = jax.nn.silu(g.astype(f32)) * y
    return y.astype(h.dtype) @ w_out

def swiglu(h, w_in, w_out):
    gt, up = jnp.split(h @ w_in, 2, axis=-1)
    return (jax.nn.silu(gt) * up) @ w_out

def moe_swiglu(h, router_w, w_in, w_out):
    f32 = jnp.float32
    bsz, s, d = h.shape
    t = bsz * s
    xt = h.reshape(t, d)
    logits = (xt @ router_w).astype(f32)
    top_logit, top_idx = lax.top_k(logits, TOP_K)
    gates = jax.nn.softmax(top_logit, axis=-1)
    e_flat = top_idx.reshape(-1)
    tok_flat = jnp.repeat(jnp.arange(t, dtype=jnp.int32), TOP_K)
    g_flat = gates.reshape(-1)
    order = jnp.argsort(e_flat)
    e_sorted = e_flat[order]
    counts = jnp.bincount(e_flat, length=N_EXPERTS)
    padded = (counts + MOE_BLOCK - 1) // MOE_BLOCK * MOE_BLOCK
    start = jnp.cumsum(counts) - counts
    pend = jnp.cumsum(padded)
    pstart = pend - padded
    dest = pstart[e_sorted] + (jnp.arange(t * TOP_K) - start[e_sorted])
    n_blocks = -(-(t * TOP_K) // MOE_BLOCK) + N_EXPERTS
    cap = n_blocks * MOE_BLOCK
    slot_tok = jnp.zeros((cap,), jnp.int32).at[dest].set(tok_flat[order])
    slot_gate = jnp.zeros((cap,), f32).at[dest].set(g_flat[order])
    block_exp = jnp.clip(jnp.searchsorted(pend, jnp.arange(n_blocks) * MOE_BLOCK, side="right"),
                         0, N_EXPERTS - 1)

    def expert_block(args):
        toks, eid = args
        xb = xt[toks]
        gt, up = jnp.split(xb @ w_in[eid], 2, axis=-1)
        return (jax.nn.silu(gt) * up) @ w_out[eid]

    yb = lax.map(expert_block, (slot_tok.reshape(n_blocks, MOE_BLOCK), block_exp))
    y = jnp.zeros((t, d), f32).at[slot_tok].add(yb.reshape(cap, d).astype(f32) * slot_gate[:, None])
    return y.astype(h.dtype).reshape(bsz, s, d)

def setup_inputs(seed: int = 0) -> dict:
    key = jax.random.key(seed)
    ks = iter(jax.random.split(key, 48))

    def nrm(shape, scale):
        return jax.random.normal(next(ks), shape, jnp.float32) * scale

    def gain(shape):
        return 1.0 + nrm(shape, 0.02)

    D = D_MODEL
    x = nrm((BATCH, SEQ, D), 1.0)
    c = nrm((BATCH, D), 1.0)
    offset = jax.random.randint(next(ks), (BATCH,), 0, 4096, dtype=jnp.int32)
    positions = offset[:, None] + jnp.arange(SEQ, dtype=jnp.int32)[None, :]
    dt = jnp.exp(jax.random.uniform(next(ks), (N_SSD, SSD_HEADS), jnp.float32,
                                    math.log(1e-3), math.log(1e-1)))
    ssd_dt_bias = dt + jnp.log(-jnp.expm1(-dt))
    ssd_a_log = jnp.log(jax.random.uniform(next(ks), (N_SSD, SSD_HEADS), jnp.float32, 1.0, 16.0))
    return {
        "x": x,
        "c": c,
        "positions": positions,
        "ada_w": nrm((DEPTH, D, 6 * D), 0.3 * D ** -0.5),
        "ada_b": nrm((DEPTH, 6 * D), 0.02),
        "norm1_g": gain((DEPTH, D)),
        "norm2_g": gain((DEPTH, D)),
        "ssd_w_in": nrm((N_SSD, D, SSD_IN_DIM), D ** -0.5),
        "ssd_conv_w": nrm((N_SSD, SSD_CONV, SSD_CONV_DIM), SSD_CONV ** -0.5),
        "ssd_conv_b": nrm((N_SSD, SSD_CONV_DIM), 0.02),
        "ssd_dt_bias": ssd_dt_bias,
        "ssd_a_log": ssd_a_log,
        "ssd_d": gain((N_SSD, SSD_HEADS)),
        "ssd_norm_g": gain((N_SSD, SSD_D_INNER)),
        "ssd_w_out": nrm((N_SSD, SSD_D_INNER, D), SSD_D_INNER ** -0.5),
        "mla_w_in": nrm((N_MLA, D, MLA_IN_DIM), D ** -0.5),
        "mla_q_norm_g": gain((N_MLA, MLA_Q_RANK)),
        "mla_kv_norm_g": gain((N_MLA, MLA_KV_RANK)),
        "mla_w_uq": nrm((N_MLA, MLA_Q_RANK, MLA_HEADS * MLA_QK), MLA_Q_RANK ** -0.5),
        "mla_w_ukv": nrm((N_MLA, MLA_KV_RANK, MLA_HEADS * (MLA_NOPE + MLA_V)), MLA_KV_RANK ** -0.5),
        "mla_q_nope_g": gain((N_MLA, MLA_NOPE)),
        "mla_q_rope_g": gain((N_MLA, MLA_ROPE)),
        "mla_k_nope_g": gain((N_MLA, MLA_NOPE)),
        "mla_k_rope_g": gain((N_MLA, MLA_ROPE)),
        "mla_w_out": nrm((N_MLA, MLA_HEADS * MLA_V, D), (MLA_HEADS * MLA_V) ** -0.5),
        "ret_w_in": nrm((N_RET, D, RET_IN_DIM), D ** -0.5),
        "ret_norm_g": gain((N_RET, RET_HEADS * RET_V)),
        "ret_w_out": nrm((N_RET, RET_HEADS * RET_V, D), (RET_HEADS * RET_V) ** -0.5),
        "ffn_w_in": nrm((N_DENSE, D, 2 * FFN_DIM), D ** -0.5),
        "ffn_w_out": nrm((N_DENSE, FFN_DIM, D), FFN_DIM ** -0.5),
        "router_w": nrm((N_MOE, D, N_EXPERTS), D ** -0.5),
        "moe_w_in": nrm((N_MOE, N_EXPERTS, D, 2 * EXPERT_DIM), D ** -0.5),
        "moe_w_out": nrm((N_MOE, N_EXPERTS, EXPERT_DIM, D), EXPERT_DIM ** -0.5),
    }

def reference(x, c, positions, ada_w, ada_b, norm1_g, norm2_g,
              ssd_w_in, ssd_conv_w, ssd_conv_b, ssd_dt_bias, ssd_a_log, ssd_d, ssd_norm_g, ssd_w_out,
              mla_w_in, mla_q_norm_g, mla_kv_norm_g, mla_w_uq, mla_w_ukv,
              mla_q_nope_g, mla_q_rope_g, mla_k_nope_g, mla_k_rope_g, mla_w_out,
              ret_w_in, ret_norm_g, ret_w_out,
              ffn_w_in, ffn_w_out, router_w, moe_w_in, moe_w_out):
    for i in range(DEPTH):
        mod = c @ ada_w[i] + ada_b[i]
        shift1, scale1, gate1, shift2, scale2, gate2 = jnp.split(mod[:, None, :], 6, axis=-1)
        h = rms_norm(x, norm1_g[i]) * (1.0 + scale1) + shift1
        kind, j = i % N_MIXERS, i // N_MIXERS
        if kind == 0:
            y = ssd_mixer(h, ssd_w_in[j], ssd_conv_w[j], ssd_conv_b[j], ssd_dt_bias[j],
                          ssd_a_log[j], ssd_d[j], ssd_norm_g[j], ssd_w_out[j])
        elif kind == 1:
            y = mla_mixer(h, positions, mla_w_in[j], mla_q_norm_g[j], mla_kv_norm_g[j],
                          mla_w_uq[j], mla_w_ukv[j], mla_q_nope_g[j], mla_q_rope_g[j],
                          mla_k_nope_g[j], mla_k_rope_g[j], mla_w_out[j])
        else:
            y = retention_mixer(h, positions, ret_w_in[j], ret_norm_g[j], ret_w_out[j])
        x = x + gate1 * y
        h = rms_norm(x, norm2_g[i]) * (1.0 + scale2) + shift2
        if i % 2 == 0:
            y = swiglu(h, ffn_w_in[i // 2], ffn_w_out[i // 2])
        else:
            y = moe_swiglu(h, router_w[i // 2], moe_w_in[i // 2], moe_w_out[i // 2])
        x = x + gate2 * y
    return x


_drawn_inputs = setup_inputs


def setup_inputs(seed=0):
    import zlib

    import numpy as np

    out = dict(_drawn_inputs(seed))
    spreads = {}
    factors = {'norm1_g': 4.725,
     'norm2_g': 3.406,
     'ssd_conv_b': 4.401,
     'ssd_d': 180.627,
     'ssd_norm_g': 4.673,
     'mla_q_norm_g': 8.0,
     'mla_kv_norm_g': 8.0,
     'mla_q_nope_g': 8.0,
     'mla_q_rope_g': 8.0,
     'mla_k_nope_g': 8.0,
     'mla_k_rope_g': 8.0}
    for name, (base, spread) in spreads.items():
        noise = np.random.default_rng([zlib.crc32(name.encode()), seed]).standard_normal(out[name].shape)
        drawn = base * np.exp(spread * noise) if base else spread * noise
        out[name] = __import__('jax').numpy.asarray(drawn.astype(out[name].dtype))
    for name, factor in factors.items():
        out[name] = (out[name] * factor).astype(out[name].dtype)
    return out
```

```python
import numpy as np
import concourse.bass as bass
import concourse.mybir as mybir

F32, F32R, I32, U32 = mybir.dt.float32, mybir.dt.float32r, mybir.dt.int32, mybir.dt.uint32
ALU, ACT, AX = mybir.AluOpType, mybir.ActivationFunctionType, mybir.AxisListType

P = 128
D, SEQ, DEPTH, EPS = 1024, 256, 2, 1e-6
KD, NB = D // P, SEQ // P
HALF = 64
DI, GROUPS, STATE, HEADS, HDIM, TAPS = 2048, 4, 128, 32, 64, 4
HPG = HEADS // GROUPS
GW = HPG * HDIM
CONV = DI + 2 * GROUPS * STATE
CT_N = CONV // P
MH, NOPE, ROPE, VD, RANK = 8, 128, 64, 128, 256
QK = NOPE + ROPE
SCALE = QK ** -0.5
FFN, NEXP, ED = 2816, 8, 3584
TILE = 512
CHUNK = 2048
PIECE = CHUNK // 2
RAW_SLOTS, SPLIT_SLOTS, AHEAD = 3, 4, 3
BIG = 4096.0

_CONST = [("ident", P), ("upto_all", 2 * P), ("before", P), ("late_none", 2 * P), ("iota", 2 * P), ("inv_freq", ROPE // 2),
          ("mhalf", 8)]
CONST_AT, _at = {}, 0
for _name, _width in _CONST:
    CONST_AT[_name] = (_at, _at + _width)
    _at += _width
NCONST = _at


def shape_constants():
    c = np.zeros((P, NCONST), np.float32)
    row, col = np.arange(P)[:, None], np.arange(P)[None, :]
    upto = (row <= col).astype(np.float32)

    def put(name, value):
        c[:, CONST_AT[name][0]:CONST_AT[name][1]] = value
    put("ident", np.eye(P))
    put("upto_all", np.concatenate([upto, np.ones((P, P))], 1))
    put("before", row < col)
    late = np.where((row < HALF) & (col >= HALF), -1e30, 0.0)
    put("late_none", np.concatenate([late, np.zeros((P, P))], 1))
    put("iota", np.arange(2 * P)[None, :])
    put("inv_freq", (np.float32(10000.0) ** (-np.arange(0, ROPE, 2, dtype=np.float32) / np.float32(ROPE)))[None, :])
    put("mhalf", -0.5)
    return c


class Tally:

    def __init__(self):
        self.seen, self.done, self.newest, self.reg, self.step = {}, {}, None, None, {}

    def value(self, sem, base):
        per = self.step.get(id(sem), 0)
        return base if self.reg is None or per == 0 else self.reg * per + base

    def next(self, sem, k=1):
        self.seen[id(sem)] = self.seen.get(id(sem), 0) + k
        return sem, self.value(sem, self.seen[id(sem)])

    def skip(self, sem, k=1):
        self.seen[id(sem)] = self.seen.get(id(sem), 0) + k

    def count(self, sem):
        return self.seen.get(id(sem), 0)

    def made(self, sem):
        self.done[id(sem)] = self.done.get(id(sem), 0) + 1
        self.newest = (sem, self.value(sem, self.done[id(sem)]))
        return sem, 1

    def last(self):
        return self.newest

    def enter(self, reg, steps):
        self.reg, self.step, self.entry = reg, {id(s): k for s, k in steps}, (dict(self.seen), dict(self.done))

    def leave(self, rounds):
        for now, was in ((self.seen, self.entry[0]), (self.done, self.entry[1])):
            for k, v in list(now.items()):
                moved = v - was.get(k, 0)
                assert moved in (0, self.step.get(k, 0)), "a loop's body must advance each count by its step"
                now[k] = was.get(k, 0) + moved * rounds
        self.reg, self.newest = None, None


def rows_of(w, k0, k, c0, n):
    return w[k0 * P:(k0 + k) * P, c0:c0 + n].rearrange("(k p) n -> p k n", p=P)


def build(nc, x, c, positions, ada_w, ada_b, norm1_g, norm2_g, ssd_w_in, ssd_conv_w, ssd_conv_b, ssd_dt_bias,
          ssd_a_log, ssd_d, ssd_norm_g, ssd_w_out, mla_w_in, mla_q_norm_g, mla_kv_norm_g, mla_w_uq, mla_w_ukv,
          mla_q_nope_g, mla_q_rope_g, mla_k_nope_g, mla_k_rope_g, mla_w_out, ffn_w_in, ffn_w_out, router_w,
          moe_w_in, moe_w_out, consts_in, out):
    top = [16512]

    def place(name, shape, dtype=F32, at=None):
        size = int(np.prod(shape[1:])) * 4
        if at is None:
            at, top[0] = top[0], (top[0] + size + 31) // 32 * 32
        assert at + size <= 229344, name
        return nc.alloc_sbuf_tensor_at(name, shape, dtype, offset=at)

    consts = place("consts", [P, NCONST])
    cols = place("cols", [P, 278])
    ada_rows = place("ada_rows", [96, P])
    modc = place("modc", [P, DEPTH, 2, 2, KD])
    head_rows = place("head_rows", [P, 3, HEADS])
    rope_gain = place("rope_gain", [P, 2, ROPE])
    pos_i = place("pos_i", [P, NB], I32)
    small = place("small", [P, 48])
    hnorm = place("hnorm", [P, 50])
    xres = place("xres", [P, NB, D])
    hT = place("hT", [P, KD, SEQ])
    hTh = place("hTh", [P, KD, SEQ], F32R)
    hTl = place("hTl", [P, KD, SEQ], F32R)
    gates = place("gates", [P, 2, D])
    acc = place("acc", [P, CHUNK])
    raw = place("raw", [P, RAW_SLOTS, CHUNK])
    whi = place("whi", [P, SPLIT_SLOTS, PIECE], F32R)
    wlo = place("wlo", [P, SPLIT_SLOTS, PIECE], F32R)
    arena = top[0]
    assert arena <= 131200, arena

    def area(start, items):
        tiles, at = [], arena + start
        for name, shape, dtype in items:
            tiles.append(place(name, shape, dtype, at=at))
            at += (int(np.prod(shape[1:])) * 4 + 31) // 32 * 32
        return tiles

    SSD_AREA = [("xs", [P, NB, DI], F32), ("zs", [P, NB, DI], F32), ("BT", [P, GROUPS, SEQ], F32),
                ("CT", [P, GROUPS, SEQ], F32), ("decay", [P, 2, HPG, P], F32), ("cbm", [P, 2, 3, P], F32),
                ("xdt", [P, 2, GW], F32), ("xend", [P, GW], F32), ("xskip", [P, 2, GW], F32), ("wide", [P, GW], F32),
                ("dts", [P, 5, NB, HEADS], F32)]
    xs, zs, BT, CT, decay, cbm, xdt, xend, xskip, wide, dts = area(0, SSD_AREA)
    YG = sum(int(np.prod(s[1:])) * 4 for _, s, _ in SSD_AREA)
    ygTh, ygTl = area(YG, [("ygTh", [P, DI // P, SEQ], F32R), ("ygTl", [P, DI // P, SEQ], F32R)])
    xn, rows_tmp, w_dt = area(YG, [("xn", [P, NB, D], F32), ("rows_tmp", [96, 2, P], F32),
                                   ("w_dt", [P, KD, HEADS], F32)])
    upad, conv, xsT = area(YG + 16384, [("upad", [P, 2, 2, SEQ + 4], F32), ("conv", [P, 2, 2, SEQ], F32),
                                        ("xsT", [P, 2, 2, SEQ], F32)])

    XN2 = 229344 - arena - NB * D * 4
    aTh, aTl, sil, act_nat = area(0, [("aTh", [P, FFN // P, SEQ], F32R), ("aTl", [P, FFN // P, SEQ], F32R),
                                      ("sil", [P, NB, TILE], F32), ("act_nat", [P, NB, TILE], F32)])
    xn2, = area(XN2, [("xn2", [P, NB, D], F32)])
    latn, latTh, latTl = area(0, [("latn", [P, NB, 2 * RANK], F32), ("latTh", [P, 4, SEQ], F32R),
                                  ("latTl", [P, 4, SEQ], F32R)])
    oTh, oTl = area(0, [("oTh", [P, MH, SEQ], F32R), ("oTl", [P, MH, SEQ], F32R)])
    q_nat, kv_nat, sq, qr, kpe, kz, trig, rot, qnT, knT, qrT, krT = area(16384, [
        ("q_nat", [P, NB, MH, QK], F32), ("kv_nat", [P, NB, MH, NOPE + VD], F32), ("sq", [P, NB, MH, QK], F32),
        ("qr", [P, NB, MH, ROPE], F32), ("kpe", [P, NB, ROPE], F32), ("kz", [P, NB, 2, P], F32),
        ("trig", [P, 6, NB, ROPE // 2], F32), ("rot", [P, 2, MH, ROPE // 2], F32),
        ("qnT", [P, MH, SEQ], F32), ("knT", [P, MH, SEQ], F32), ("qrT", [P, MH // 2, SEQ], F32),
        ("krT", [P, 2, SEQ], F32)])
    w_kpe, = area(16384 + 12288 + 16384, [("w_kpe", [P, KD, ROPE], F32)])
    assert 16384 + 12288 + 16384 + 12288 + 4096 + 512 + 2048 + 1536 + 2048 + 8192 + 8192 + 4096 + 2048 <= XN2
    scores, probsT, sstat = area(16384 + 12288 + 16384, [
        ("scores", [P, 2, 3 * P], F32), ("probsT", [P, 2, 3 * P], F32), ("sstat", [P, 2, 8], F32)])
    (h2n, y_moe, xeTh, xeTl, eTh, eTl, ye, place_m, place_g, placeT, esil, e_nat, w_router, route, top8, topi, posm,
     gates8, flag) = area(0, [
         ("h2n", [P, NB, D], F32), ("y_moe", [P, NB, D], F32), ("xeTh", [P, KD, P], F32R), ("xeTl", [P, KD, P], F32R),
         ("eTh", [P, ED // P, P], F32R), ("eTl", [P, ED // P, P], F32R), ("ye", [P, D], F32),
         ("place_m", [P, NB, P], F32), ("place_g", [P, NB, P], F32), ("placeT", [P, SEQ], F32),
         ("esil", [P, 2, TILE], F32), ("e_nat", [P, 2, TILE], F32), ("w_router", [P, KD, NEXP], F32),
         ("route", [P, 8, NB, NEXP], F32), ("top8", [P, NB, 8], F32), ("topi", [P, NB, 8], U32),
         ("posm", [P, NB, NEXP + 1], F32), ("gates8", [P, NB, NEXP + 1], F32), ("flag", [P, 1], I32)])

    bank = [nc.alloc_psum_tensor(f"bank{i}", [P, TILE], F32) for i in range(8)]
    tbank, ybank = bank[4:6], bank[6:8]

    def const(name, a=0, b=None):
        lo, hi = CONST_AT[name]
        return consts[:, lo + a:(lo + b if b is not None else hi)]
    ident = const("ident")
    upto, ones = const("upto_all", 0, P), const("upto_all", P, 2 * P)
    ADA_COL, CONVW_COL, MISC_COL = 0, 96, 192
    misc = {}
    at = MISC_COL
    for name, n in (("c", 8), ("norm1", 16), ("norm2", 16), ("conv_b", 24), ("ssd_norm", 16), ("qkv_norm", 4),
                    ("q_nope", 1), ("k_nope", 1)):
        misc[name] = at
        at += n

    def col(at, n=1):
        return cols[:, at:at + n]

    stream, first = [], {}

    def weights(phase, views):
        first.setdefault(phase, 2 * sum(kind == "w" for kind, _ in stream))
        for v in views:
            stream.append(("w", v))

    def ada_chunk(i):
        layer, third, k = i // 24, i // 8 % 3, i % 8
        return "ada", ada_w[layer][k * P:(k + 1) * P, third * CHUNK:(third + 1) * CHUNK]
    ada_next = [0]

    def ada(n=1):
        for _ in range(n):
            stream.append(ada_chunk(ada_next[0]))
            ada_next[0] += 1

    ada(8)
    w = ssd_w_in[0]
    conv_cols = [DI + DI + 256 * i for i in range(4)] + [DI + 256 * i for i in range(8)]
    weights("conv", [rows_of(w, 0, KD, c0, 256) for c0 in conv_cols])
    for n in range(4):
        for half in range(2):
            ada()
            weights("z", [rows_of(w, 4 * half, 4, n * TILE, TILE)])
    for k in range(8):
        weights("ssd_out", [rows_of(ssd_w_out[0], 2 * k, 2, 0, D)])
        ada((0, 2, 2, 1, 1, 1, 1, 0)[k])
    ffn_tiles = [(n * TILE, min(TILE, FFN - n * TILE)) for n in range(-(-FFN // TILE))]
    j = 0
    for c0, n in ffn_tiles:
        for side in (0, FFN):
            kc = CHUNK // n
            for k0 in range(0, KD, kc):
                weights("ffn_in", [rows_of(ffn_w_in[0], k0, kc, side + c0, n)])
                j += 1
                ada(1 if 2 <= j < 10 or 14 <= j < 22 else 0)
    for k in range(FFN // P // 2):
        weights("ffn_out", [rows_of(ffn_w_out[0], 2 * k, 2, 0, D)])
        ada(1 if 1 <= k < 9 else 0)
    assert ada_next[0] == 48
    MOD_AFTER_TILE = {2: 3, len(ffn_tiles) - 1: 4}
    for k0 in (0, 4):
        weights("mla_in", [rows_of(mla_w_in[0], k0, 4, 0, TILE)])
    for n in range(2):
        weights("mla_uq", [rows_of(mla_w_uq[0], 0, 2, n * 768, 768)])
    for n in range(2):
        weights("mla_ukv", [rows_of(mla_w_ukv[0], 0, 2, n * D, D)])
    for k in range(4):
        weights("mla_out", [rows_of(mla_w_out[0], 2 * k, 2, 0, D)])
    NS = len(stream)
    piece_chunk = [s for s, (kind, _) in enumerate(stream) if kind == "w" for _ in range(2)]
    w_before = np.cumsum([0] + [kind == "w" for kind, _ in stream])
    first["moe"] = len(piece_chunk)
    MOE_TILES, MOE_K = ED // TILE, ED // P
    MOE_CHUNKS = MOE_TILES * 4 + MOE_K // 2
    assert MOE_CHUNKS % RAW_SLOTS == 0 and 2 * MOE_CHUNKS % SPLIT_SLOTS == 0
    moe_in = moe_w_in[0].rearrange("e d n -> (e d) n")
    moe_out = moe_w_out[0].rearrange("e d n -> (e d) n")

    def moe_view(e, j):
        if j < MOE_TILES * 4:
            n, side, k0 = j // 4, j % 4 // 2, j % 2 * 4
            v = moe_in[bass.ds(e * D + k0 * P, 4 * P), side * ED + n * TILE:side * ED + (n + 1) * TILE]
        else:
            v = moe_out[bass.ds(e * ED + (j - MOE_TILES * 4) * 2 * P, 2 * P), :]
        return v.rearrange("(k p) n -> p k n", p=P)

    T_LAST, G_FIRST, G_SECOND = 3, 8, 12

    def shaped(tile, slot, view):
        k, n = view.shape[1], view.shape[2]
        return tile[:, slot, 0:k * n].rearrange("p (k n) -> p k n", k=k)

    def half_of(tile, slot, half, view):
        size = view.shape[1] * view.shape[2] // 2
        return tile[:, slot, half * size:(half + 1) * size]

    sem = nc.alloc_semaphore
    consts_landed, vectors_landed, x_landed = sem("consts_landed"), sem("vectors_landed"), sem("x_landed")
    raw_landed = [sem(f"raw_landed{i}") for i in range(RAW_SLOTS)]
    out_stored = sem("out_stored")
    hi_ready, lo_ready, weights_used, ada_done = sem("hi_ready"), sem("lo_ready"), sem("weights_used"), sem("ada_done")
    t_full, t_drained = sem("t_full"), sem("t_drained")
    dve_step, act_step, pool_step = sem("dve_step"), sem("act_step"), sem("pool_step")
    x_ready, cols_ready = sem("x_ready"), sem("cols_ready")
    ssq_ready, rstd_ready, xn_ready, hi_made, lo_made = (sem(s) for s in
                                                         ("ssq_ready", "rstd_ready", "xn_ready", "hi_made", "lo_made"))
    act_read, dve_read = sem("act_read"), sem("dve_read")
    gate_ready = sem("gate_ready")
    xsT_ready, bc_ready, dt_ready, decay_ready = sem("xsT_ready"), sem("bc_ready"), sem("dt_ready"), sem("decay_ready")
    taps_in, taps_ready, exp_ready, soft_in = sem("taps_in"), sem("taps_ready"), sem("exp_ready"), sem("soft_in")
    r_full, e_ready, m_ready = sem("r_full"), sem("e_ready"), sem("m_ready")
    xdt_ready, y_full, y_used, yg_ready, yn_ready = (sem(s) for s in
                                                    ("xdt_ready", "y_full", "y_used", "yg_ready", "yn_ready"))
    small_landed, kpe_landed, router_landed = sem("small_landed"), sem("kpe_landed"), sem("router_landed")
    gate_read, silu_ready, a_ready = sem("gate_read"), sem("silu_ready"), sem("a_ready")
    lat_ready, latn_ready, kpe_full, q_ready, k_ready = (sem(s) for s in
                                                        ("lat_ready", "latn_ready", "kpe_full", "q_ready", "k_ready"))
    sqrt_in, sqrt_ready, trig_in, trig_ready = sem("sqrt_in"), sem("sqrt_ready"), sem("trig_in"), sem("trig_ready")
    sq_ready, gap_ready = sem("sq_ready"), sem("gap_ready")
    s_full, s_ready, p_exp, p_ready, o_full = (sem(s) for s in ("s_full", "s_ready", "p_exp", "p_ready", "o_full"))
    zeroed = sem("zeroed")
    mask_ready, placed, ye_ready, flag_ready = sem("mask_ready"), sem("placed"), sem("ye_ready"), sem("flag_ready")

    THIRDS = (("shift1", "scale1"), ("gate1", "shift2"), ("scale2", "gate2"))
    N_VECTORS = 11

    def mod_fills(third):
        return 1 if third % 3 == 0 else 3
    XS_FILLS = 1 + 1 + KD // 2 + 1 + 1 + DI // P // 2
    ROUND = 1.5 * 2.0 ** 23
    TWO_PI = [6.28125]
    TWO_PI.append(float(np.float32(np.floor((2 * np.pi - TWO_PI[0]) * 2.0 ** 20) / 2.0 ** 20)))
    TWO_PI.append(2 * np.pi - sum(TWO_PI))
    PI_IN = 3.1415925

    def lat_block(b):
        return xn2[:, b, 0:4 * P].rearrange("p (k t) -> p k t", k=4)

    def used_after(base):
        return weights_used, first["moe"] + (base + NEXP) * 2 * MOE_CHUNKS

    block_cm = nc.Block()
    block = block_cm.__enter__()

    @block.sync
    def _(sp):
        sp.dma_start(xres[:, :, :], x[0].rearrange("(b p) d -> p b d", p=P)).then_inc(x_landed, 16)
        for s, (kind, view) in enumerate(stream):
            if s >= RAW_SLOTS:
                was = s - RAW_SLOTS
                if stream[was][0] == "ada":
                    sp.wait_ge(ada_done, was + 1 - int(w_before[was]))
                else:
                    sp.wait_ge(lo_ready, 2 * int(w_before[was]) + 2)
            dst = raw[:, s % RAW_SLOTS, :] if kind == "ada" else shaped(raw, s % RAW_SLOTS, view)
            sp.dma_start(dst, view).then_inc(raw_landed[s % RAW_SLOTS], 16)
        def experts(base):
            with sp.Fori(0, NEXP) as e:
                for j in range(MOE_CHUNKS):
                    s = NS + base * MOE_CHUNKS + j
                    was = first["moe"] + 2 * (base * MOE_CHUNKS + j - RAW_SLOTS) + 2
                    sp.wait_ge(lo_ready, e * (2 * MOE_CHUNKS) + was)
                    sp.dma_start(shaped(raw, s % RAW_SLOTS, moe_view(e, j)), moe_view(e, j)).then_inc(
                        raw_landed[s % RAW_SLOTS], 16)
        experts(0)
        sp.wait_ge(flag_ready, 1)
        with sp.If(sp.value_load(flag[0:1, 0:1]) > P):
            experts(NEXP)
        sp.wait_ge(x_ready, NB * 2 * DEPTH)
        sp.dma_start(out[0].rearrange("(b p) d -> p b d", p=P), xres[:, :, :]).then_inc(out_stored, 16)
        sp.wait_ge(out_stored, 16)

    class Place:
        def __init__(self):
            self.piece = self.chunk = 0
            self.reg = None
            self.base = 0

    def piece_tile(tile, p, view):
        return tile[:, p % SPLIT_SLOTS, 0:view.shape[1] * view.shape[2] // 2]

    def act_split(act, at, last):
        while at.piece <= last:
            p = at.piece
            s = piece_chunk[p]
            if p % 2 == 0:
                act.wait_ge(raw_landed[s % RAW_SLOTS], 16 * (s // RAW_SLOTS + 1))
            if p >= SPLIT_SLOTS:
                act.wait_ge(weights_used, p - SPLIT_SLOTS + 1)
            act.activation(piece_tile(whi, p, stream[s][1]), half_of(raw, s % RAW_SLOTS, p % 2, stream[s][1]),
                           ACT.Copy).then_inc(hi_ready, 1)
            at.piece += 1

    def dve_split(dve, at, last):
        while at.piece <= last:
            p = at.piece
            s = piece_chunk[p]
            while at.chunk < s:
                dve_ada(dve, at)
            dve.wait_ge(hi_ready, p + 1)
            dve.tensor_tensor(piece_tile(wlo, p, stream[s][1]), half_of(raw, s % RAW_SLOTS, p % 2, stream[s][1]),
                              piece_tile(whi, p, stream[s][1]).bitcast(F32), ALU.subtract).then_inc(lo_ready, 1)
            at.piece += 1
            at.chunk = s + p % 2

    def dve_ada(dve, at):
        s = at.chunk
        i = s - int(w_before[s])
        dve.wait_ge(raw_landed[s % RAW_SLOTS], 16 * (s // RAW_SLOTS + 1))
        w_k, c_k = raw[:, s % RAW_SLOTS, :], col(misc["c"] + i % KD)
        if i % KD == 0:
            dve.tensor_scalar(acc[:, :], w_k, c_k, None, ALU.mult).then_inc(ada_done, 1)
        else:
            dve.wait_ge(ada_done, i)
            dve.scalar_tensor_tensor(acc[:, :], w_k, c_k, acc[:, :], ALU.mult, ALU.add).then_inc(ada_done, 1)
        at.chunk = s + 1

    def moe_piece_view(j):
        return moe_view(0, j // 2)

    def act_split_moe(act, at, last):
        while at.piece <= last:
            j = at.piece
            s, p = NS + at.base * MOE_CHUNKS + j // 2, first["moe"] + at.base * 2 * MOE_CHUNKS + j
            if j % 2 == 0:
                act.wait_ge(raw_landed[s % RAW_SLOTS], at.reg * (16 * MOE_CHUNKS // RAW_SLOTS) + 16 * (s // RAW_SLOTS + 1))
            act.wait_ge(weights_used, at.reg * (2 * MOE_CHUNKS) + (p - SPLIT_SLOTS + 1))
            act.activation(whi[:, p % SPLIT_SLOTS, :], raw[:, s % RAW_SLOTS, j % 2 * PIECE:(j % 2 + 1) * PIECE],
                           ACT.Copy).then_inc(hi_ready, 1)
            at.piece += 1

    def dve_split_moe(dve, at, last):
        while at.piece <= last:
            j = at.piece
            s, p = NS + at.base * MOE_CHUNKS + j // 2, first["moe"] + at.base * 2 * MOE_CHUNKS + j
            dve.wait_ge(hi_ready, at.reg * (2 * MOE_CHUNKS) + (p + 1))
            dve.tensor_tensor(wlo[:, p % SPLIT_SLOTS, :], raw[:, s % RAW_SLOTS, j % 2 * PIECE:(j % 2 + 1) * PIECE],
                              whi[:, p % SPLIT_SLOTS, :].bitcast(F32), ALU.subtract).then_inc(lo_ready, 1)
            at.piece += 1

    def used(at, j):
        return weights_used, at.reg * (2 * MOE_CHUNKS) + (first["moe"] + at.base * 2 * MOE_CHUNKS + j + 1)

    MOE_FILLS = 4 + MOE_TILES + 1 + 2
    MOE_STEPS = [(t_full, MOE_FILLS), (t_drained, MOE_FILLS), (gate_read, MOE_TILES), (silu_ready, MOE_TILES),
                 (a_ready, MOE_TILES), (hi_made, MOE_TILES + 2), (ye_ready, 1), (placed, 1)]

    @block.tensor
    def _(pe):
        n = Tally()

        def t_bank():
            f = n.done.get(id(t_full), 0)
            n.started = f
            if f >= 2:
                pe.wait_ge(t_drained, n.value(t_drained, f - 1))
            return tbank[f % 2]

        def mod(third):
            pe.wait_ge(ada_done, KD * (third + 1))
            halves = THIRDS[third % 3]
            t = t_bank()
            i = 0
            for h in (0, 1):
                if not halves[h].startswith("gate"):
                    for k in range(KD):
                        last = pe.matmul(t[:, i:i + 1], acc[:, (h * KD + k) * P:(h * KD + k + 1) * P], ones[:, 0:1],
                                         start=True, stop=True)
                        i += 1
            last.then_inc(*n.made(t_full))
            for h in (0, 1):
                if halves[h].startswith("gate"):
                    for k0 in (0, 4):
                        t = t_bank()
                        for k in range(k0, k0 + 4):
                            o, row = t[:, (k - k0) * P:(k - k0 + 1) * P], third // 3 * 48 + third % 3 * 16 + h * KD + k
                            pe.matmul(o, ones, acc[:, (h * KD + k) * P:(h * KD + k + 1) * P], start=True, stop=False)
                            last = pe.matmul(o, ident[0:96, row:row + 1].to_broadcast([96, P]), ada_rows[:, :],
                                             start=False, stop=True)
                        last.then_inc(*n.made(t_full))

        def norm_to_T(src):
            pe.wait_ge(*n.next(xn_ready, NB))
            for i in range(KD // 2):
                t = t_bank()
                for j in range(2):
                    for b in range(NB):
                        k = 2 * i + j
                        last = pe.transpose(t[:, j * SEQ + b * P:j * SEQ + (b + 1) * P],
                                            src[:, b, k * P:(k + 1) * P], ident)
                last.then_inc(*n.made(t_full))

        def transposes(views):
            t = t_bank()
            for i, v in enumerate(views):
                last = pe.transpose(t[:, i * P:(i + 1) * P], v, ident)
            last.then_inc(*n.made(t_full))
            return n.done[id(t_full)]

        def wait_fill(fill):
            pe.wait_ge(t_drained, n.value(t_drained, fill))

        def natural(p, lhs, k0, kcount, ktot, width, outs, ready=None):
            pe.wait_ge(lo_ready, ready if ready is not None else p + 1)
            h, l = whi[:, p % SPLIT_SLOTS, :], wlo[:, p % SPLIT_SLOTS, :]
            for kk in range(kcount):
                k = k0 + kk
                for b, views in enumerate(outs):
                    xh, xl = lhs(k, b)
                    for i, (xx, ww) in enumerate(((xh, h), (xh, l), (xl, h))):
                        for view, c0, c1 in views:
                            last = pe.matmul(view, xx, ww[:, kk * width + c0:kk * width + c1],
                                             start=(k == 0 and i == 0), stop=(k == ktot - 1 and i == 2))
            last.then_inc(weights_used, 1)

        def blk(tile):
            return lambda k, b: tile[:, k, b * P:(b + 1) * P]

        def pair(hi, lo, k0=0):
            return lambda k, b: (hi[:, k0 + k, b * P:(b + 1) * P], lo[:, k0 + k, b * P:(b + 1) * P])

        wide_outs = [[(bank[2 * b + i][:, :], i * TILE, (i + 1) * TILE) for i in range(2)] for b in range(NB)]

        pe.wait_ge(consts_landed, 16)
        pe.wait_ge(vectors_landed, 16 * N_VECTORS)
        t = t_bank()
        pe.transpose(t[:, 0:96], ada_rows[:, :], ident[0:96, 0:96])
        pe.transpose(t[:, 96:192], rows_tmp[:, 0, :], ident[0:96, 0:96])
        pe.transpose(t[:, 192:278], rows_tmp[0:86, 1, :], ident[0:86, 0:86]).then_inc(*n.made(t_full))

        mod(0)
        norm_to_T(xn)
        pe.wait_ge(*n.next(lo_made, KD // 2))
        t = t_bank()
        pe.wait_ge(small_landed, 16 * 7)
        for b in range(NB):
            for k in range(KD):
                last = pe.matmul(t[:, b * HEADS:(b + 1) * HEADS], hT[:, k, b * P:(b + 1) * P], w_dt[:, k, :],
                                 start=(k == 0), stop=(k == KD - 1))
        last.then_inc(*n.made(t_full))
        for ch in range(CT_N // 2 + 2):
            if ch < CT_N // 2:
                if ch >= 2:
                    pe.wait_ge(*n.next(act_read))
                for half in range(2):
                    p = first["conv"] + 2 * ch + half
                    pe.wait_ge(lo_ready, p + 1)
                    for kk in range(KD // 2):
                        k = half * KD // 2 + kk
                        for i in range(2):
                            wa = kk * 256 + i * P
                            wh, wl = (tile[:, p % SPLIT_SLOTS, wa:wa + P] for tile in (whi, wlo))
                            for j, (ww, xx) in enumerate(((wh, hTh), (wh, hTl), (wl, hTh))):
                                last = pe.matmul(bank[ch % 2 * 2 + i][:, 0:SEQ], ww, xx[:, k, :],
                                                 start=(k == 0 and j == 0), stop=(k == KD - 1 and j == 2))
                    last.then_inc(weights_used, 1)
            if ch == 2:
                pe.wait_ge(*n.next(dt_ready))
                t = t_bank()
                pe.matmul(t[:, 0:NB * HEADS], upto, dts[:, 1].rearrange("p b h -> p (b h)"), start=True, stop=True)
                pe.matmul(t[:, NB * HEADS:2 * NB * HEADS], ones, dts[:, 1].rearrange("p b h -> p (b h)"), start=True,
                          stop=True).then_inc(*n.made(t_full))
            if ch - 2 >= 4:
                pe.wait_ge(*n.next(xsT_ready))
                transposes([xsT[:, ch % 2, i, b * P:(b + 1) * P] for b in range(NB) for i in range(2)])
        for m in range(4):
            pe.wait_ge(*n.next(act_read))
            for q in range(4):
                natural(first["z"] + 4 * m + q, pair(hTh, hTl), 2 * q, 2, KD, TILE,
                        [[(bank[m % 2 * 2 + b][:, :], 0, TILE)] for b in range(NB)])
        mod(1)
        pe.wait_ge(*n.next(bc_ready, 4))
        for step in range(2 * GROUPS + 2):
            if step < 2 * GROUPS:
                g, b = step // 2, step % 2
                if b == 0:
                    t = t_bank()
                    pe.matmul(t[:, 0:SEQ], BT[:, g, 0:P], CT[:, g, :], start=True, stop=True)
                    pe.matmul(t[:, SEQ:SEQ + P], BT[:, g, P:SEQ], CT[:, g, P:SEQ], start=True,
                              stop=True).then_inc(*n.made(t_full))
                if step:
                    pe.wait_ge(*n.next(e_ready))
                for h in range(HPG):
                    last = pe.matmul(ybank[h // 4][:, h % 4 * P:(h % 4 + 1) * P],
                                     dts[:, 1, b, g * HPG + h:g * HPG + h + 1].to_broadcast([P, P]), upto,
                                     start=True, stop=True)
                last.then_inc(*n.made(r_full))
            if 1 <= step <= 2 * GROUPS:
                v = step - 1
                g, b = v // 2, v % 2
                if v == 0:
                    pe.wait_ge(*n.next(act_read, 2))
                if v >= 2:
                    pe.wait_ge(*n.next(y_used))
                pe.wait_ge(*n.next(xdt_ready))
                pe.wait_ge(*n.next(m_ready))
                if b == 1:
                    pe.matmul(bank[2][:, :], cbm[:, g % 2, 1, :], xend[:, :], start=True, stop=True)
                for h in range(HPG):
                    last = pe.matmul(bank[b][:, h * HDIM:(h + 1) * HDIM], decay[:, b, h, :],
                                     xdt[:, b, h * HDIM:(h + 1) * HDIM], start=True, stop=True)
                last.then_inc(*n.made(y_full))
            if step >= 2:
                v = step - 2
                g, b = v // 2, v % 2
                pe.wait_ge(*n.next(yn_ready))
                transposes([zs[:, b, g * GW + i * P:g * GW + (i + 1) * P] for i in range(GW // P)])
        pe.wait_ge(*n.next(y_used, 2))
        pe.wait_ge(*n.next(lo_made, 2 * GROUPS))
        for k in range(DI // P):
            natural(first["ssd_out"] + k, pair(ygTh, ygTl), k, 1, DI // P, D, wide_outs)
        mod(2)

        norm_to_T(xn2)
        pe.wait_ge(*n.next(lo_made, KD // 2))
        p = first["ffn_in"]
        tile_fill = {}
        for m, (c0, width) in enumerate(ffn_tiles):
            kc = PIECE // width
            for side in (0, 1):
                if side == 0 and m:
                    pe.wait_ge(*n.next(gate_read))
                if side == 1 and m:
                    pe.wait_ge(*n.next(a_ready))
                    for b in range(NB):
                        tile_fill[m - 1] = transposes([act_nat[:, b, i * P:(i + 1) * P] for i in range(TILE // P)])
                for k0 in range(0, KD, kc):
                    natural(p, pair(hTh, hTl), k0, kc, KD, width,
                            [[(bank[2 * side + b][:, 0:width], 0, width)] for b in range(NB)])
                    p += 1
            if m in MOD_AFTER_TILE:
                mod(MOD_AFTER_TILE[m])
        pe.wait_ge(*n.next(gate_read))
        pe.wait_ge(*n.next(a_ready))
        for b in range(NB):
            tile_fill[len(ffn_tiles) - 1] = transposes([act_nat[:, b, i * P:(i + 1) * P]
                                                        for i in range(ffn_tiles[-1][1] // P)])
        for k in range(FFN // P):
            if k % 4 == 0:
                wait_fill(tile_fill[k // 4])
            natural(first["ffn_out"] + k, pair(aTh, aTl), k, 1, FFN // P, D, wide_outs)
        mod(5)

        norm_to_T(xn2)
        pe.wait_ge(*n.next(lo_made, KD // 2))
        for q in range(4):
            natural(first["mla_in"] + q, pair(hTh, hTl), 2 * q, 2, KD, TILE,
                    [[(bank[b][:, :], 0, TILE)] for b in range(NB)])
        pe.wait_ge(kpe_landed, 16)
        for b in range(NB):
            for k in range(KD):
                last = pe.matmul(bank[2][:, b * ROPE:(b + 1) * ROPE], hT[:, k, b * P:(b + 1) * P], w_kpe[:, k, :],
                                 start=(k == 0), stop=(k == KD - 1))
        last.then_inc(*n.made(kpe_full))
        pe.wait_ge(*n.next(latn_ready))
        for b in range(NB):
            transposes([latn[:, b, i * P:(i + 1) * P] for i in range(4)])
        pe.wait_ge(*n.next(lo_made, NB))
        pe.wait_ge(*n.next(dve_read))
        for m in range(4):
            if m:
                pe.wait_ge(*n.next(act_read))
                pe.wait_ge(*n.next(dve_read))
            name, width, k_lat = ("mla_uq", 768, 0) if m < 2 else ("mla_ukv", D, 2)
            outs = [[(bank[2 * b][:, :], 0, TILE), (bank[2 * b + 1][:, 0:width - TILE], TILE, width)]
                    for b in range(NB)]
            for k in range(2):
                natural(first[name] + m % 2 * 2 + k, pair(latTh, latTl, k_lat), k, 1, 2, width, outs)
        for i in range(MH // 2):
            if i == 0:
                pe.wait_ge(*n.next(q_ready))
            transposes([q_nat[:, b, 2 * i + j, 0:NOPE] for j in range(2) for b in range(NB)])
        for i in range(MH // 2):
            if i == 0:
                pe.wait_ge(*n.next(k_ready))
            transposes([kv_nat[:, b, 2 * i + j, 0:NOPE] for j in range(2) for b in range(NB)])
        pe.wait_ge(*n.next(q_ready))
        for i in range(2):
            transposes([qr[:, b, 4 * i + 2 * j:4 * i + 2 * j + 2, :].rearrange("p h d -> p (h d)") for j in range(2)
                        for b in range(NB)])
        pe.wait_ge(*n.next(k_ready))
        transposes([kz[:, b, j, :] for j in range(2) for b in range(NB)])
        pe.wait_ge(*n.next(act_read))
        pe.wait_ge(*n.next(dve_read))
        wait_fill(n.done[id(t_full)])
        probs_fill = {}
        for step in range(MH + 2):
            if step < MH:
                h = step
                if h >= 2:
                    pe.wait_ge(*n.next(s_ready))
                for b in range(NB):
                    o = bank[h % 2][:, b * P:b * P + (b + 1) * P]
                    pe.matmul(o, qnT[:, h, b * P:(b + 1) * P], knT[:, h, 0:(b + 1) * P], start=True, stop=False)
                    last = pe.matmul(o, qrT[:, h // 2, b * P:(b + 1) * P], krT[:, h % 2, 0:(b + 1) * P], start=False,
                                     stop=True)
                last.then_inc(*n.made(s_full))
            if 1 <= step <= MH:
                pe.wait_ge(*n.next(p_ready))
                probs_fill[step - 1] = transposes([scores[:, (step - 1) % 2, i * P:(i + 1) * P] for i in range(3)])
            if step >= 2:
                h = step - 2
                if h >= 2:
                    pe.wait_ge(*n.next(lo_made))
                wait_fill(probs_fill[h])
                o = ybank[h % 2]
                pe.matmul(o[:, 0:P], kv_nat[:, 0, h, NOPE:], probsT[:, h % 2, 0:P], start=True, stop=True)
                for kb in range(NB):
                    last = pe.matmul(o[:, P:SEQ], kv_nat[:, kb, h, NOPE:], probsT[:, h % 2, (1 + kb) * P:(2 + kb) * P],
                                     start=(kb == 0), stop=(kb == 1))
                last.then_inc(*n.made(o_full))
        pe.wait_ge(*n.next(s_ready, 2))
        pe.wait_ge(*n.next(lo_made, 2))
        for k in range(MH):
            natural(first["mla_out"] + k, pair(oTh, oTl), k, 1, MH, D, wide_outs)

        norm_to_T(xn2)
        pe.wait_ge(*n.next(lo_made, KD // 2))
        for b in range(NB):
            for i in range(2):
                transposes([hT[:, 4 * i + j, b * P:(b + 1) * P] for j in range(4)])
        pe.wait_ge(router_landed, 16)
        t = t_bank()
        for b in range(NB):
            for k in range(KD):
                last = pe.matmul(t[:, b * NEXP:(b + 1) * NEXP], hT[:, k, b * P:(b + 1) * P], w_router[:, k, :],
                                 start=(k == 0), stop=(k == KD - 1))
        last.then_inc(*n.made(t_full))
        pe.wait_ge(*n.next(mask_ready))
        t = t_bank()
        mask = route[:, 0]
        pe.matmul(t[:, 0:NEXP], const("before"), mask[:, 0, :], start=True, stop=True)
        pe.matmul(t[:, NEXP:2 * NEXP], ones, mask[:, 0, :], start=True, stop=False)
        pe.matmul(t[:, NEXP:2 * NEXP], const("before"), mask[:, 1, :], start=False, stop=True)
        pe.matmul(t[:, 2 * NEXP:3 * NEXP], ones, mask[:, 0, :], start=True, stop=False)
        pe.matmul(t[:, 2 * NEXP:3 * NEXP], ones, mask[:, 1, :], start=False, stop=True).then_inc(*n.made(t_full))

        def gather(half):
            t = t_bank()
            for j in range(4):
                k = 4 * half + j
                for b in range(NB):
                    last = pe.matmul(t[:, j * P:(j + 1) * P], h2n[:, b, k * P:(k + 1) * P], place_m[:, b, :],
                                     start=(b == 0), stop=(b == NB - 1))
            last.then_inc(*n.made(t_full))

        def combine(i):
            t = t_bank()
            pe.matmul(t[:, :], placeT[:, i // 2 * P:(i // 2 + 1) * P], ye[:, i % 2 * TILE:(i % 2 + 1) * TILE],
                      start=True, stop=True).then_inc(*n.made(t_full))

        def experts(base):
            pe.wait_ge(*n.next(placed))
            for i in range(2):
                last = pe.matmul(ybank[i][:, :], placeT[:, 0:P], h2n[:, 0, i * TILE:(i + 1) * TILE], start=True,
                                 stop=True)
            last.then_inc(*n.made(o_full))
            gather(0)
            gather(1)
            at = Place()
            at.base = base
            with pe.Fori(0, NEXP) as e:
                at.reg = e
                n.enter(e, MOE_STEPS)

                def expert_piece(j, lhs, k0, kcount, ktot, width, outs):
                    p = first["moe"] + base * 2 * MOE_CHUNKS + j
                    natural(p, lhs, k0, kcount, ktot, width, outs, ready=e * (2 * MOE_CHUNKS) + (p + 1))
                wait_fill(n.done[id(t_full)])
                tile_fill = {}
                lhs_x = lambda k, b: (xeTh[:, k, :], xeTl[:, k, :])
                lhs_a = lambda k, b: (eTh[:, k, :], eTl[:, k, :])
                for m in range(MOE_TILES):
                    if m != 1:
                        pe.wait_ge(gate_read, n.value(gate_read, n.count(gate_read) + max(m - 1, 0)))
                    for q in range(4):
                        expert_piece(8 * m + q, lhs_x, 2 * q, 2, KD, TILE, [[(bank[m % 2][:, :], 0, TILE)]])
                    if m == 0:
                        pe.wait_ge(*n.next(ye_ready))
                        combine(0)
                        combine(1)
                    else:
                        pe.wait_ge(*n.next(a_ready))
                        tile_fill[m - 1] = transposes([e_nat[:, (m - 1) % 2, i * P:(i + 1) * P]
                                                       for i in range(TILE // P)])
                    if m in (1, 2):
                        combine(m + 1)
                    if m == 3:
                        transposes([place_g[:, b, :] for b in range(NB)])
                    for q in range(4):
                        expert_piece(8 * m + 4 + q, lhs_x, 2 * q, 2, KD, TILE, [[(bank[2 + m % 2][:, :], 0, TILE)]])
                for k in range(MOE_K):
                    if k % 4 == 0:
                        wait_fill(tile_fill[k // 4])
                    expert_piece(8 * MOE_TILES + k, lhs_a, k, 1, MOE_K, D,
                                 [[(ybank[i][:, :], i * TILE, (i + 1) * TILE) for i in range(2)]])
                    if k == T_LAST:
                        pe.wait_ge(*n.next(a_ready))
                        tile_fill[MOE_TILES - 1] = transposes([e_nat[:, (MOE_TILES - 1) % 2, i * P:(i + 1) * P]
                                                               for i in range(TILE // P)])
                    if k == G_FIRST:
                        pe.wait_ge(*n.next(placed))
                        gather(0)
                    if k == G_SECOND:
                        gather(1)
                n.skip(gate_read, MOE_TILES)
            n.leave(NEXP)
            pe.wait_ge(*n.next(ye_ready))
            for i in range(4):
                combine(i)

        experts(0)
        pe.wait_ge(flag_ready, 1)
        with pe.If(pe.value_load(flag[0:1, 0:1]) > P):
            experts(NEXP)

    @block.scalar
    def _(act):
        n = Tally()
        at = Place()

        act.dma_start(consts[:, :], consts_in).then_inc(consts_landed, 16)
        act.dma_start(ada_rows[:, :], ada_b.rearrange("l (k p) -> (l k) p", p=P)).then_inc(vectors_landed, 16)
        act.dma_start(rows_tmp[:, 0, :], ssd_conv_w[0].rearrange("t (k p) -> (t k) p", p=P)).then_inc(
            vectors_landed, 16)
        for name, src in (("c", c), ("norm1", norm1_g), ("norm2", norm2_g), ("conv_b", ssd_conv_b),
                          ("ssd_norm", ssd_norm_g), ("q_nope", mla_q_nope_g), ("k_nope", mla_k_nope_g),
                          ("qkv_norm", mla_q_norm_g), ("qkv_norm2", mla_kv_norm_g)):
            r = misc["qkv_norm"] + 2 - MISC_COL if name == "qkv_norm2" else misc[name] - MISC_COL
            rows = src.shape[0] * src.shape[1] // P
            act.dma_start(rows_tmp[r:r + rows, 1, :], src.rearrange("l (k p) -> (l k) p", p=P)).then_inc(
                vectors_landed, 16)
        act.dma_start(w_dt[:, :, :], rows_of(ssd_w_in[0], 0, KD, 2 * DI + 2 * GROUPS * STATE, HEADS)).then_inc(
            small_landed, 16)
        for i, src in enumerate((ssd_dt_bias, ssd_a_log, ssd_d)):
            act.dma_start(head_rows[:, i, :], src.to_broadcast([P, HEADS])).then_inc(small_landed, 16)
        for i, src in enumerate((mla_q_rope_g, mla_k_rope_g)):
            act.dma_start(rope_gain[:, i, :], src.to_broadcast([P, ROPE])).then_inc(small_landed, 16)
        act.dma_start(pos_i[:, :], positions.rearrange("o (b p) -> p (o b)", p=P), allow_slow_non_contiguous=True).then_inc(small_landed, 16)

        def norm(next_piece, scratch, before_split=None):
            for b in range(NB):
                act.activation(scratch[:, b, :], xres[:, b, :], ACT.Square,
                               accum_out=small[:, b:b + 1]).then_inc(*n.made(ssq_ready))
            if next_piece < first["moe"]:
                act_split(act, at, next_piece + AHEAD - 1)
            for i in range(KD // 2):
                act.wait_ge(*n.next(t_drained))
                act.activation(hTh[:, 2 * i:2 * i + 2, :], hT[:, 2 * i:2 * i + 2, :], ACT.Copy).then_inc(
                    *n.made(hi_made))

        def tb():
            return tbank[(n.count(t_full) - 1) % 2]

        def skip_fills(k):
            n.skip(t_full, k)
            n.skip(t_drained, k)

        act.wait_ge(x_landed, 16)
        act.wait_ge(small_landed, 16 * 7)
        act.activation(head_rows[:, 1, :], head_rows[:, 1, :], ACT.Exp).then_inc(*n.made(exp_ready))
        n.skip(t_drained, 2)
        norm(first["conv"], xn)
        n.skip(t_full, 6)
        act.wait_ge(*n.next(soft_in))
        act.activation(wide[:, 0:64], wide[:, 0:64], ACT.Exp).then_inc(*n.made(exp_ready))
        skip_fills(1)
        n.skip(t_full, 1)
        for ch in range(CT_N // 2 + 1):
            if ch < CT_N // 2:
                f = 16 + 2 * ch if ch < 4 else 2 * ch - 8
                q = first["conv"] + 2 * ch + 1
                act_split(act, at, q + AHEAD)
                act.wait_ge(weights_used, q + 1)
                if ch >= 2:
                    act.wait_ge(*n.last())
                for i in range(2):
                    act.activation(upad[:, ch % 2, i, TAPS - 1:TAPS - 1 + SEQ], bank[ch % 2 * 2 + i][:, 0:SEQ], ACT.Copy)
                    ins = act.activation(conv[:, ch % 2, i, :], bank[ch % 2 * 2 + i][:, 0:SEQ], ACT.Identity,
                                         bias=col(misc["conv_b"] + f + i), scale=col(CONVW_COL + 3 * CT_N + f + i))
                ins.then_inc(*n.made(act_read))
            if ch == 3:
                act.wait_ge(*n.next(dt_ready, 2))
                act.activation(dts[:, 3, :, :], dts[:, 3, :, :], ACT.Exp).then_inc(*n.made(exp_ready))
            if ch >= 1:
                j = ch - 1
                act.wait_ge(*n.next(taps_ready))
                if j >= 6:
                    act.wait_ge(*n.next(t_full))
                dst = BT[:, 2 * j:2 * j + 2, :] if j < 2 else CT[:, 2 * j - 4:2 * j - 2, :] if j < 4 else xsT[:, j % 2]
                act.activation(dst, conv[:, j % 2], ACT.Silu).then_inc(*n.made(bc_ready if j < 4 else xsT_ready))
        n.skip(t_full, 2)
        n.skip(t_drained, 9)
        for m in range(4):
            q = first["z"] + 4 * m + 3
            act_split(act, at, q + AHEAD)
            act.wait_ge(weights_used, q + 1)
            for b in range(NB):
                ins = act.activation(zs[:, b, m * TILE:(m + 1) * TILE], bank[m % 2 * 2 + b][:, :], ACT.Silu)
            ins.then_inc(*n.made(act_read))
        skip_fills(3)
        for step in range(2 * GROUPS + 2):
            if step < 2 * GROUPS:
                n.skip(t_drained, 1 if step % 2 == 0 else 0)
                act.wait_ge(*n.next(e_ready))
                act.activation(decay[:, step % 2], decay[:, step % 2], ACT.Exp).then_inc(*n.made(exp_ready))
            if 1 <= step <= 2 * GROUPS:
                v = step - 1
                act.wait_ge(*n.next(yg_ready))
                act.activation(bank[3][:, :], zs[:, v % 2, v // 2 * GW:(v // 2 + 1) * GW], ACT.Square,
                               accum_out=small[:, 8 + v:9 + v]).then_inc(*n.made(ssq_ready))
            if step >= 2:
                v = step - 2
                act.wait_ge(*n.next(t_drained))
                act.activation(ygTh[:, v // 2 * 4:v // 2 * 4 + 4, v % 2 * P:(v % 2 + 1) * P],
                               wide[:, :].rearrange("p (k t) -> p k t", k=4), ACT.Copy).then_inc(*n.made(hi_made))
        n.skip(t_full, GROUPS + 2 * GROUPS)
        act_split(act, at, first["ssd_out"] + DI // P - 1)
        skip_fills(3)

        act.wait_ge(*n.next(x_ready, NB))
        norm(first["ffn_in"], xn2)
        n.skip(t_full, 4)
        q = first["ffn_in"] - 1

        def split_T(m, b, width):
            act.wait_ge(*n.next(t_full))
            act.activation(aTh[:, 4 * m:4 * m + width // P, b * P:(b + 1) * P],
                           tb()[:, 0:width].rearrange("p (k t) -> p k t", k=width // P),
                           ACT.Copy).then_inc(*n.made(hi_made))
        for m, (c0, width) in enumerate(ffn_tiles):
            q += KD * width // PIECE
            act_split(act, at, q + AHEAD)
            act.wait_ge(weights_used, q + 1)
            if m:
                act.wait_ge(*n.next(a_ready))
            for b in range(NB):
                ins = act.activation(sil[:, b, 0:width], bank[b][:, 0:width], ACT.Silu)
            ins.then_inc(*n.made(gate_read))
            if m:
                for b in range(NB):
                    split_T(m - 1, b, TILE)
            q += KD * width // PIECE
            act_split(act, at, q + AHEAD)
            if m in MOD_AFTER_TILE:
                n.skip(t_full, mod_fills(MOD_AFTER_TILE[m]))
        for b in range(NB):
            split_T(len(ffn_tiles) - 1, b, ffn_tiles[-1][1])
        n.skip(t_full, 3)
        n.skip(t_drained, 2 * len(ffn_tiles) - 2 + 2 + sum(mod_fills(third) for third in (3, 4, 5)))
        act_split(act, at, first["ffn_out"] + FFN // P - 1)

        act.wait_ge(*n.next(x_ready, NB))
        act.dma_start(w_kpe[:, :, :], rows_of(mla_w_in[0], 0, KD, 2 * RANK, ROPE)).then_inc(kpe_landed, 16)
        norm(first["mla_in"], xn2)
        n.skip(t_full, 4)
        act.wait_ge(*n.next(trig_in))
        act.activation(trig[:, 0:2], trig[:, 2:4], ACT.Sin).then_inc(*n.made(trig_ready))
        q = first["mla_in"] + 3
        act_split(act, at, q + AHEAD)
        act.wait_ge(weights_used, q + 1)
        for b in range(NB):
            for i in range(2):
                ins = act.activation(xn2[:, b, i * RANK:(i + 1) * RANK], bank[b][:, i * RANK:(i + 1) * RANK], ACT.Square,
                                     accum_out=small[:, 8 + 2 * b + i:9 + 2 * b + i])
        ins.then_inc(*n.made(ssq_ready))
        for b in range(NB):
            act.wait_ge(*n.next(t_drained))
            act.activation(latTh[:, :, b * P:(b + 1) * P], lat_block(b), ACT.Copy).then_inc(*n.made(hi_made))
        n.skip(t_full, 2)
        act.wait_ge(*n.next(sqrt_in))
        act.activation(hnorm[:, 48:50], hnorm[:, 48:50], ACT.Sqrt).then_inc(*n.made(sqrt_ready))
        n.skip(dve_read, 1)
        for m in range(4):
            name, width = ("mla_uq", 768) if m < 2 else ("mla_ukv", D)
            q = first[name] + m % 2 * 2 + 1
            act_split(act, at, q + AHEAD)
            act.wait_ge(weights_used, q + 1)
            dst = (q_nat if m < 2 else kv_nat)[:, 0].rearrange("p h d -> p (h d)")
            for i in range(2):
                a, b_ = i * TILE, min((i + 1) * TILE, width)
                ins = act.activation(dst[:, m % 2 * width + a:m % 2 * width + b_], bank[i][:, 0:b_ - a], ACT.Copy)
            ins.then_inc(*n.made(act_read))
            if m % 2:
                act.wait_ge(*n.last())
                act.wait_ge(*n.next(dve_read, 2))
                if m == 1:
                    act.activation(sq[:, :, :, :], q_nat[:, :, :, :], ACT.Square).then_inc(*n.made(sq_ready))
                else:
                    act.wait_ge(*n.next(sqrt_in))
                    act.activation(hnorm[:, 0:32], hnorm[:, 0:32], ACT.Sqrt).then_inc(*n.made(sqrt_ready))
                    act.activation(sq[:, :, :, 0:NOPE], kv_nat[:, :, :, 0:NOPE], ACT.Square).then_inc(
                        *n.made(sq_ready))
                    act.wait_ge(*n.next(sqrt_in))
                    act.activation(hnorm[:, 32:48], hnorm[:, 32:48], ACT.Sqrt).then_inc(*n.made(sqrt_ready))
        skip_fills(11)
        for step in range(MH + 2):
            if step < MH:
                h = step
                act.wait_ge(*n.next(s_ready))
                for b in range(NB):
                    ins = act.activation(scores[:, h % 2, b * P:(2 * b + 1) * P], scores[:, h % 2, b * P:(2 * b + 1) * P],
                                         ACT.Exp, bias=sstat[:, h % 2, 2 + b:3 + b], scale=SCALE,
                                         accum_out=sstat[:, h % 2, 4 + b:5 + b])
                ins.then_inc(*n.made(p_exp))
            if step >= 2:
                h = step - 2
                act.wait_ge(*n.next(o_full))
                act.activation(oTh[:, h, :], ybank[h % 2][:, 0:SEQ], ACT.Copy).then_inc(*n.made(hi_made))
        skip_fills(MH)
        act_split(act, at, first["mla_out"] + MH - 1)

        act.wait_ge(*n.next(x_ready, NB))
        act.dma_start(w_router[:, :, :], rows_of(router_w[0], 0, KD, 0, NEXP)).then_inc(router_landed, 16)
        norm(first["moe"], xn2)
        skip_fills(5)
        n.skip(t_full, 5)
        act.wait_ge(*n.next(gap_ready))
        act.activation(route[:, 6, :, 0:1], route[:, 6, :, 0:1], ACT.Exp).then_inc(*n.made(exp_ready))

        def split_gather(half):
            act.wait_ge(*n.next(t_full))
            act.activation(xeTh[:, 4 * half:4 * half + 4, :], tb()[:, :].rearrange("p (k t) -> p k t", k=4),
                           ACT.Copy).then_inc(*n.made(hi_made))

        def experts(base):
            at = Place()
            at.base = base
            split_gather(0)
            split_gather(1)
            act.wait_ge(*n.next(o_full))
            with act.Fori(0, NEXP) as e:
                at.reg = e
                n.enter(e, MOE_STEPS)
                for m in range(MOE_TILES):
                    if m == 0:
                        act_split_moe(act, at, AHEAD - 1)
                        act.wait_ge(*used(at, -1))
                        for i in range(2):
                            ins = act.activation(ye[:, i * TILE:(i + 1) * TILE], ybank[i][:, :], ACT.Copy)
                        ins.then_inc(*n.made(ye_ready))
                    act_split_moe(act, at, 8 * m + 3 + AHEAD)
                    act.wait_ge(*used(at, 8 * m + 3))
                    if m >= 2:
                        act.wait_ge(*n.next(a_ready))
                    act.activation(esil[:, m % 2, :], bank[m % 2][:, :], ACT.Silu).then_inc(*n.made(gate_read))
                    if m == 0:
                        n.skip(t_full, 2)
                    else:
                        split_tile(act, n, m - 1)
                        n.skip(t_full, 1 if m in (1, 2, 3) else 0)
                    act_split_moe(act, at, 8 * m + 7 + AHEAD)
                n.skip(a_ready, 2)
                w_out = 8 * MOE_TILES
                act_split_moe(act, at, w_out + T_LAST + AHEAD)
                split_tile(act, n, MOE_TILES - 1)
                act_split_moe(act, at, w_out + G_FIRST + AHEAD)
                split_gather(0)
                act_split_moe(act, at, w_out + G_SECOND + AHEAD)
                split_gather(1)
                act_split_moe(act, at, 2 * MOE_CHUNKS - 1)
                at.piece = 0
            n.leave(NEXP)
            act.wait_ge(*used_after(base))
            for i in range(2):
                ins = act.activation(ye[:, i * TILE:(i + 1) * TILE], ybank[i][:, :], ACT.Copy)
            ins.then_inc(*n.made(ye_ready))
            n.skip(t_full, 4)

        def split_tile(act, n, m):
            act.wait_ge(*n.next(t_full))
            act.activation(eTh[:, 4 * m:4 * m + 4, :], tb()[:, :].rearrange("p (k t) -> p k t", k=4),
                           ACT.Copy).then_inc(*n.made(hi_made))
        experts(0)
        act.wait_ge(flag_ready, 1)
        with act.If(act.value_load(flag[0:1, 0:1]) > P):
            experts(NEXP)

    @block.vector
    def _(dve):
        n = Tally()
        at = Place()
        rows8 = lambda v: v.rearrange("p (h d) -> p h d", h=HPG)

        def tb():
            return tbank[(n.count(t_full) - 1) % 2]

        def spread(v, width):
            return v.unsqueeze(2).to_broadcast([P, v.shape[1], width])

        def mod(third):
            l = third // 3
            halves = THIRDS[third % 3]
            dve.wait_ge(*n.next(t_full))
            t, i, scaled = tb(), 0, None
            cols_of = [h for h in (0, 1) if not halves[h].startswith("gate")]
            for h in cols_of:
                sub, kind = int(halves[h][-1]) - 1, 0 if halves[h].startswith("scale") else 1
                dst = modc[:, l, sub, kind, :]
                bias = col(l * 48 + third % 3 * 16 + h * KD, KD)
                dve.tensor_tensor(dst, t[:, i * KD:(i + 1) * KD], bias, ALU.add).then_inc(
                    *n.made(t_drained if h == cols_of[-1] else dve_step))
                if kind == 0:
                    scaled = (dst, col(misc["norm1" if sub == 0 else "norm2"] + l * KD, KD))
                i += 1
            if scaled:
                dve.wait_ge(*n.last())
                dve.scalar_tensor_tensor(scaled[0], scaled[0], 1.0, scaled[1], ALU.add, ALU.mult).then_inc(
                    *n.made(dve_step))
            for h in (0, 1):
                if halves[h].startswith("gate"):
                    for i in range(2):
                        dve.wait_ge(*n.next(t_full))
                        dve.tensor_copy(gates[:, int(halves[h][-1]) - 1, i * TILE:(i + 1) * TILE], tb()[:, :]).then_inc(
                            *n.made(t_drained))

        def norm(l, sub, dst, next_piece):
            dve.wait_ge(*n.next(rstd_ready))
            for b in range(NB):
                dve.tensor_scalar(dst[:, b, :], xres[:, b, :], small[:, 4 + b:5 + b], None, ALU.mult).then_inc(
                    *n.made(xn_ready))
            if next_piece < first["moe"]:
                dve_split(dve, at, next_piece + AHEAD - 1)
            dve.wait_ge(*n.last())
            for i in range(KD // 2 + 1):
                if i < KD // 2:
                    dve.wait_ge(*n.next(t_full))
                    for j in range(2):
                        k = 2 * i + j
                        ins = dve.tensor_scalar(hT[:, k, :], tb()[:, j * SEQ:(j + 1) * SEQ], modc[:, l, sub, 0, k:k + 1],
                                                modc[:, l, sub, 1, k:k + 1], ALU.mult, ALU.add)
                    ins.then_inc(*n.made(t_drained))
                if i >= 1:
                    k = 2 * i - 2
                    dve.wait_ge(*n.next(hi_made))
                    dve.wait_ge(*n.last())
                    dve.tensor_tensor(hTl[:, k:k + 2, :], hT[:, k:k + 2, :], hTh[:, k:k + 2, :].bitcast(F32),
                                      ALU.subtract).then_inc(*n.made(lo_made))

        def residual(q, sub, scratch):
            dve.wait_ge(weights_used, q + 1)
            for i in range(5):
                if i < 4:
                    b, half = i // 2, i % 2
                    dve.tensor_tensor(scratch[:, b, half * TILE:(half + 1) * TILE], bank[i][:, :],
                                      gates[:, sub, half * TILE:(half + 1) * TILE], ALU.mult).then_inc(
                        *n.made(dve_step))
                if i:
                    b, half = (i - 1) // 2, (i - 1) % 2
                    cut = slice(half * TILE, (half + 1) * TILE)
                    dve.wait_ge(*n.last())
                    dve.tensor_tensor(xres[:, b, cut], xres[:, b, cut], scratch[:, b, cut], ALU.add).then_inc(
                        *n.made(x_ready if half else dve_step))

        dve.memset(upad[:, :, :, 0:TAPS - 1], 0.0).then_inc(*n.made(dve_step))
        dve.wait_ge(*n.next(t_full))
        dve.tensor_copy(cols[:, :], tb()[:, 0:278]).then_inc(*n.made(t_drained))
        dve.wait_ge(*n.last())
        while at.chunk < KD:
            dve_ada(dve, at)
        mod(0)

        norm(0, 0, xn, first["conv"])
        flat = lambda i: dts[:, i].rearrange("p b h -> p (b h)")
        e_, d_, s_, p_ = (wide[:, i * 64:(i + 1) * 64] for i in range(4))
        dve.wait_ge(*n.next(t_full))
        dve.tensor_tensor(dts[:, 0], tb()[:, 0:64].rearrange("p (b h) -> p b h", b=NB),
                          head_rows[:, 0, :].unsqueeze(1).to_broadcast([P, NB, HEADS]), ALU.add).then_inc(
            *n.made(t_drained))
        dve.wait_ge(*n.last())
        dve.scalar_tensor_tensor(e_, flat(0), -1.0, flat(0), ALU.mult, ALU.min).then_inc(*n.made(soft_in))
        dve_split(dve, at, first["conv"] + 3)
        dve.wait_ge(*n.next(exp_ready, 2))

        def step(ins, sem_=None):
            ins.then_inc(*n.made(sem_ or dve_step))
            dve.wait_ge(*n.last())
        step(dve.tensor_scalar(d_, e_, 2.0, None, ALU.add))
        step(dve.reciprocal(d_, d_))
        step(dve.tensor_tensor(e_, e_, d_, ALU.mult))
        step(dve.tensor_tensor(s_, e_, e_, ALU.mult))
        step(dve.tensor_scalar(p_, s_, 1.0 / 15, None, ALU.mult))
        for odd in (13, 11, 9, 7, 5, 3):
            step(dve.scalar_tensor_tensor(p_, p_, 1.0 / odd, s_, ALU.add, ALU.mult))
        step(dve.scalar_tensor_tensor(p_, p_, 1.0, e_, ALU.add, ALU.mult))
        step(dve.tensor_scalar(flat(0), flat(0), 0.0, None, ALU.max))
        step(dve.scalar_tensor_tensor(flat(0), p_, 2.0, flat(0), ALU.mult, ALU.add))
        dve.scalar_tensor_tensor(dts[:, 1], dts[:, 0], -1.0, head_rows[:, 1, :].unsqueeze(1).to_broadcast([P, NB, HEADS]),
                                 ALU.mult, ALU.mult).then_inc(*n.made(dt_ready))
        for ch in range(CT_N // 2 + 2):
            if ch < CT_N // 2:
                f = 16 + 2 * ch if ch < 4 else 2 * ch - 8
                dve_split(dve, at, first["conv"] + 2 * ch + 1 + AHEAD)
                dve.wait_ge(*n.next(act_read))
                for tap in range(TAPS - 1):
                    if tap:
                        dve.wait_ge(*n.last())
                    for i in range(2):
                        ins = dve.scalar_tensor_tensor(conv[:, ch % 2, i, :], upad[:, ch % 2, i, tap:tap + SEQ],
                                                       col(CONVW_COL + tap * CT_N + f + i), conv[:, ch % 2, i, :],
                                                       ALU.mult, ALU.add)
                    ins.then_inc(*n.made(taps_ready if tap == TAPS - 2 else dve_step))
            if ch == 2:
                dve.wait_ge(*n.next(t_full))
                step(dve.tensor_copy(flat(2), tb()[:, 0:64]))
                dve.tensor_tensor(dts[:, 3, 0, :], tb()[:, 64:64 + HEADS], dts[:, 2, 0, :], ALU.subtract).then_inc(
                    *n.made(t_drained))
                dve.tensor_copy(dts[:, 3, 1, :], dts[:, 2, 1, :]).then_inc(*n.made(dt_ready))
            if ch == 4:
                dve.wait_ge(*n.next(exp_ready))
                dve.tensor_tensor(dts[:, 4, 0, :], dts[:, 0, 0, :], dts[:, 3, 0, :], ALU.mult).then_inc(
                    *n.made(dt_ready))
            if ch - 2 >= 4:
                c0 = (ch - 6) * 2 * P
                dve.wait_ge(*n.next(t_full))
                dve.tensor_copy(xs[:, :, c0:c0 + 2 * P], tb()[:, :].rearrange("p (b f) -> p b f", b=NB)).then_inc(
                    *n.made(t_drained))
        n.skip(act_read, 4)
        dve_split(dve, at, first["z"] + 15 + AHEAD)
        mod(1)
        for stepno in range(2 * GROUPS + 3):
            if 2 <= stepno < 2 * GROUPS + 2:
                v = stepno - 2
                cut = zs[:, v % 2, v // 2 * GW:(v // 2 + 1) * GW]
                dve.wait_ge(*n.next(rstd_ready))
                dve.tensor_scalar(cut, cut, small[:, 40 + v:41 + v], None, ALU.mult).then_inc(*n.made(yn_ready))
            if stepno < 2 * GROUPS:
                g, b = stepno // 2, stepno % 2
                if b == 0:
                    dve.wait_ge(*n.next(t_full))
                    if g == 0:
                        dve.wait_ge(*n.last())
                    dve.tensor_tensor(cbm[:, g % 2, 0:2, :], tb()[:, 0:SEQ].rearrange("p (i t) -> p i t", i=2),
                                      const("upto_all").rearrange("p (i t) -> p i t", i=2), ALU.mult)
                    dve.tensor_tensor(cbm[:, g % 2, 2, :], tb()[:, SEQ:SEQ + P], upto, ALU.mult).then_inc(
                        *n.made(t_drained))
                dve.wait_ge(*n.next(r_full))
                for h in range(HPG):
                    hh = g * HPG + h
                    ins = dve.tensor_scalar(decay[:, b, h, :], ybank[h // 4][:, h % 4 * P:(h % 4 + 1) * P],
                                            dts[:, 2, b, hh:hh + 1], 0.0, ALU.subtract, ALU.min)
                ins.then_inc(*n.made(e_ready))
            if 1 <= stepno <= 2 * GROUPS:
                v = stepno - 1
                g, b = v // 2, v % 2
                dve.wait_ge(*n.next(y_full))
                sk = xskip[:, b, :]
                dve.tensor_tensor(sk, bank[b][:, :], sk, ALU.add).then_inc(*n.made(y_used if b == 0 else dve_step))
                if b == 1:
                    dve.tensor_tensor(rows8(bank[2][:, :]), rows8(bank[2][:, :]),
                                      spread(dts[:, 3, 1, g * HPG:(g + 1) * HPG], HDIM), ALU.mult).then_inc(
                        *n.made(dve_step))
                    dve.wait_ge(*n.last())
                    dve.tensor_tensor(sk, bank[2][:, :], sk, ALU.add).then_inc(*n.made(y_used))
                dve.wait_ge(*n.last())
                cut = zs[:, b, g * GW:(g + 1) * GW]
                dve.tensor_tensor(cut, sk, cut, ALU.mult).then_inc(*n.made(yg_ready))
            if stepno < 2 * GROUPS:
                dve.wait_ge(*n.next(exp_ready))
                dve.tensor_tensor(decay[:, stepno % 2], decay[:, stepno % 2],
                                  cbm[:, stepno // 2 % 2, 2 * (stepno % 2), :].unsqueeze(1).to_broadcast([P, HPG, P]),
                                  ALU.mult).then_inc(*n.made(m_ready))
            if stepno >= 3:
                v = stepno - 3
                dst = slice(v // 2 * 4, v // 2 * 4 + 4), slice(v % 2 * P, (v % 2 + 1) * P)
                dve.wait_ge(*n.next(hi_made))
                dve.wait_ge(*n.last())
                dve.tensor_tensor(ygTl[:, dst[0], dst[1]], wide[:, :].rearrange("p (k t) -> p k t", k=4),
                                  ygTh[:, dst[0], dst[1]].bitcast(F32), ALU.subtract).then_inc(*n.made(lo_made))
            if 2 <= stepno < 2 * GROUPS + 2:
                v = stepno - 2
                dve.wait_ge(*n.next(t_full))
                dve.wait_ge(*n.last())
                dve.tensor_tensor(wide[:, :].rearrange("p (k t) -> p k t", k=4),
                                  tb()[:, :].rearrange("p (k t) -> p k t", k=4),
                                  spread(col(misc["ssd_norm"] + v // 2 * 4, 4), P), ALU.mult).then_inc(
                    *n.made(t_drained))
        dve_split(dve, at, first["ssd_out"] + DI // P - 1)
        residual(first["ssd_out"] + DI // P - 1, 0, xn2)
        mod(2)

        norm(0, 1, xn2, first["ffn_in"])
        q = first["ffn_in"] - 1

        def split_T(m, b, width):
            dve.wait_ge(*n.next(t_full))
            dve.wait_ge(*n.next(hi_made))
            dst = slice(4 * m, 4 * m + width // P), slice(b * P, (b + 1) * P)
            dve.tensor_tensor(aTl[:, dst[0], dst[1]], tb()[:, 0:width].rearrange("p (k t) -> p k t", k=width // P),
                              aTh[:, dst[0], dst[1]].bitcast(F32), ALU.subtract).then_inc(*n.made(t_drained))
        for m, (c0, width) in enumerate(ffn_tiles):
            q += KD * width // PIECE
            dve_split(dve, at, q + AHEAD)
            if m:
                for b in range(NB):
                    split_T(m - 1, b, TILE)
            q += KD * width // PIECE
            dve_split(dve, at, q + AHEAD)
            dve.wait_ge(*n.next(gate_read))
            dve.wait_ge(weights_used, q + 1)
            for b in range(NB):
                ins = dve.tensor_tensor(act_nat[:, b, 0:width], bank[2 + b][:, 0:width], sil[:, b, 0:width], ALU.mult)
            ins.then_inc(*n.made(a_ready))
            if m in MOD_AFTER_TILE:
                mod(MOD_AFTER_TILE[m])
        for b in range(NB):
            split_T(len(ffn_tiles) - 1, b, ffn_tiles[-1][1])
        dve_split(dve, at, first["ffn_out"] + FFN // P - 1)
        residual(first["ffn_out"] + FFN // P - 1, 1, xn2)
        mod(5)

        norm(1, 0, xn2, first["mla_in"])
        tr = lambda i: trig[:, i].rearrange("p b f -> p (b f)")
        step(dve.tensor_copy(small[:, 6:8], pos_i[:, :]))
        for b in range(NB):
            step(dve.tensor_scalar(trig[:, 5, b, :], const("inv_freq"), small[:, 6 + b:7 + b], None, ALU.mult))
        step(dve.tensor_scalar(tr(4), tr(5), 1 / (2 * np.pi), ROUND, ALU.mult, ALU.add))
        step(dve.tensor_scalar(tr(4), tr(4), -ROUND, None, ALU.add))
        for part in TWO_PI:
            step(dve.scalar_tensor_tensor(tr(5), tr(4), -part, tr(5), ALU.mult, ALU.add))
        step(dve.tensor_scalar(tr(2), tr(5), PI_IN, -PI_IN, ALU.min, ALU.max))
        dve.tensor_scalar(tr(3), tr(2), 0.5, None, ALU.mult).then_inc(*n.made(trig_in))
        dve_split(dve, at, first["mla_in"] + 3 + AHEAD)
        dve.wait_ge(*n.next(rstd_ready))
        for b in range(NB):
            for i in range(2):
                ins = dve.tensor_scalar(latn[:, b, i * RANK:(i + 1) * RANK], bank[b][:, i * RANK:(i + 1) * RANK],
                                        small[:, 16 + 2 * b + i:17 + 2 * b + i], None, ALU.mult)
        ins.then_inc(*n.made(latn_ready))
        dve.wait_ge(*n.next(kpe_full))
        step(dve.tensor_copy(kpe[:, :, :], bank[2][:, 0:2 * ROPE].rearrange("p (b d) -> p b d", b=NB)), dve_read)
        kz2 = kz[:, :, 0, 0:ROPE]
        step(dve.tensor_tensor(kz2, kpe[:, :, :], kpe[:, :, :], ALU.mult))
        step(dve.tensor_reduce(hnorm[:, 48:50], kz2, AX.X, ALU.add))
        dve.tensor_scalar(hnorm[:, 48:50], hnorm[:, 48:50], 1.0 / ROPE, EPS, ALU.mult, ALU.add).then_inc(
            *n.made(sqrt_in))
        for b in range(NB + 1):
            if b < NB:
                dve.wait_ge(*n.next(t_full))
                dve.tensor_tensor(lat_block(b), tb()[:, :].rearrange("p (k t) -> p k t", k=4),
                                  spread(col(misc["qkv_norm"], 4), P), ALU.mult).then_inc(*n.made(t_drained))
            if b:
                dve.wait_ge(*n.next(hi_made))
                dve.wait_ge(*n.last())
                c = slice((b - 1) * P, b * P)
                dve.tensor_tensor(latTl[:, :, c], lat_block(b - 1), latTh[:, :, c].bitcast(F32),
                                  ALU.subtract).then_inc(*n.made(lo_made))
        dve.wait_ge(*n.next(trig_ready))
        step(dve.tensor_tensor(tr(4), tr(1), tr(1), ALU.mult))
        step(dve.tensor_scalar(tr(4), tr(4), -2.0, 1.0, ALU.mult, ALU.add))
        for m in range(4):
            name, width = ("mla_uq", 768) if m < 2 else ("mla_ukv", D)
            q = first[name] + m % 2 * 2 + 1
            dve_split(dve, at, q + AHEAD)
            dve.wait_ge(weights_used, q + 1)
            dst = (q_nat if m < 2 else kv_nat)[:, 1].rearrange("p h d -> p (h d)")
            for i in range(2):
                a, b_ = i * TILE, min((i + 1) * TILE, width)
                ins = dve.tensor_copy(dst[:, m % 2 * width + a:m % 2 * width + b_], bank[2 + i][:, 0:b_ - a])
            ins.then_inc(*n.made(dve_read))
        by_head = lambda tile, a, b_: tile[:, :, :, a:b_].rearrange("p b h d -> p (b h) d")
        dve.wait_ge(*n.next(sq_ready))
        step(dve.tensor_reduce(hnorm[:, 0:16], by_head(sq, 0, NOPE), AX.X, ALU.add))
        step(dve.tensor_reduce(hnorm[:, 16:32], by_head(sq, NOPE, QK), AX.X, ALU.add))
        step(dve.tensor_scalar(hnorm[:, 0:16], hnorm[:, 0:16], 1.0 / NOPE, EPS, ALU.mult, ALU.add))
        dve.tensor_scalar(hnorm[:, 16:32], hnorm[:, 16:32], 1.0 / ROPE, EPS, ALU.mult, ALU.add).then_inc(
            *n.made(sqrt_in))
        dve.wait_ge(*n.next(sqrt_ready, 2))
        step(dve.reciprocal(hnorm[:, 48:50], hnorm[:, 48:50]))
        step(dve.reciprocal(hnorm[:, 0:32], hnorm[:, 0:32]))
        dve.tensor_tensor(by_head(q_nat, 0, NOPE), by_head(q_nat, 0, NOPE), spread(hnorm[:, 0:16], NOPE),
                          ALU.mult).then_inc(*n.made(q_ready))
        dve.wait_ge(*n.next(sq_ready))
        step(dve.tensor_reduce(hnorm[:, 32:48], by_head(sq, 0, NOPE), AX.X, ALU.add))
        dve.tensor_scalar(hnorm[:, 32:48], hnorm[:, 32:48], 1.0 / NOPE, EPS, ALU.mult, ALU.add).then_inc(
            *n.made(sqrt_in))
        step(dve.tensor_tensor(by_head(q_nat, NOPE, QK), by_head(q_nat, NOPE, QK), spread(hnorm[:, 16:32], ROPE),
                               ALU.mult))
        step(dve.tensor_tensor(by_head(q_nat, NOPE, QK), by_head(q_nat, NOPE, QK),
                               rope_gain[:, 0, :].unsqueeze(1).to_broadcast([P, NB * MH, ROPE]), ALU.mult))
        dve.wait_ge(*n.next(sqrt_ready))
        step(dve.reciprocal(hnorm[:, 32:48], hnorm[:, 32:48]))
        dve.tensor_tensor(by_head(kv_nat, 0, NOPE), by_head(kv_nat, 0, NOPE), spread(hnorm[:, 32:48], NOPE),
                          ALU.mult).then_inc(*n.made(k_ready))

        def rotate(dst, x1, x2, sin, cos, t1, t2, half, done):
            step(dve.tensor_tensor(t1, x2, sin, ALU.mult))
            step(dve.tensor_tensor(t2, x1, sin, ALU.mult))
            step(dve.tensor_tensor(x1, x1, cos, ALU.mult))
            step(dve.tensor_tensor(x2, x2, cos, ALU.mult))
            step(dve.tensor_tensor(dst[0], x1, t1, ALU.subtract))
            step(dve.tensor_tensor(dst[1], x2, t2, ALU.add), done)
        H2 = ROPE // 2
        for b in range(NB):
            over = lambda i: trig[:, i, b, :].unsqueeze(1).to_broadcast([P, MH, H2])
            rotate((qr[:, b, :, 0:H2], qr[:, b, :, H2:ROPE]), q_nat[:, b, :, NOPE:NOPE + H2], q_nat[:, b, :, NOPE + H2:QK],
                   over(0), over(4), rot[:, 0], rot[:, 1], H2, q_ready if b else dve_step)
        for b in range(NB):
            step(dve.scalar_tensor_tensor(kpe[:, b, :], kpe[:, b, :], hnorm[:, 48 + b:49 + b], rope_gain[:, 1, :],
                                          ALU.mult, ALU.mult))
        step(dve.memset(kz[:, :, :, :], 0.0))
        rotate((kz[:, :, 0, 0:H2], kz[:, :, 0, H2:ROPE]), kpe[:, :, 0:H2], kpe[:, :, H2:ROPE], trig[:, 0], trig[:, 4],
               rot[:, 0, 0:2, :], rot[:, 1, 0:2, :], H2, dve_step)
        dve.tensor_copy(kz[:, :, 1, ROPE:P], kz[:, :, 0, 0:ROPE]).then_inc(*n.made(k_ready))
        for i in range(11):
            dve.wait_ge(*n.next(t_full))
            src = tb()[:, :].rearrange("p (h t) -> p h t", h=2)
            if i < 8:
                dst, gain = ((qnT, "q_nope"), (knT, "k_nope"))[i // 4]
                ins = dve.tensor_scalar(dst[:, 2 * (i % 4):2 * (i % 4) + 2, :], src, col(misc[gain]), None, ALU.mult)
            else:
                ins = dve.tensor_copy(qrT[:, 2 * (i - 8):2 * (i - 8) + 2, :] if i < 10 else krT[:, :, :], src)
            ins.then_inc(*n.made(t_drained))
        for stepno in range(MH + 2):
            if stepno < MH:
                h = stepno
                sc, st = scores[:, h % 2, :], sstat[:, h % 2, :]
                dve.wait_ge(*n.next(s_full))
                dve.tensor_tensor(sc[:, 0:SEQ], bank[h % 2][:, 0:SEQ], const("late_none"), ALU.add)
                step(dve.tensor_tensor(sc[:, SEQ:3 * P], bank[h % 2][:, SEQ:3 * P], const("late_none", 0, P), ALU.add))
                dve.tensor_reduce(st[:, 0:1], sc[:, 0:P], AX.X, ALU.max)
                step(dve.tensor_reduce(st[:, 1:2], sc[:, P:3 * P], AX.X, ALU.max))
                dve.tensor_scalar(st[:, 2:4], st[:, 0:2], -SCALE, None, ALU.mult).then_inc(*n.made(s_ready))
            if 1 <= stepno <= MH:
                dve.wait_ge(*n.next(t_full))
                dve.tensor_copy(probsT[:, (stepno - 1) % 2, :], tb()[:, 0:3 * P]).then_inc(*n.made(t_drained))
            if stepno < MH:
                dve.wait_ge(*n.next(p_exp))
                step(dve.reciprocal(st[:, 6:8], st[:, 4:6]))
                dve.tensor_scalar(sc[:, 0:P], sc[:, 0:P], st[:, 6:7], None, ALU.mult)
                dve.tensor_scalar(sc[:, P:3 * P], sc[:, P:3 * P], st[:, 7:8], None, ALU.mult).then_inc(
                    *n.made(p_ready))
            if stepno >= 2:
                h2 = stepno - 2
                dve.wait_ge(*n.next(hi_made))
                dve.tensor_tensor(oTl[:, h2, :], ybank[h2 % 2][:, 0:SEQ], oTh[:, h2, :].bitcast(F32),
                                  ALU.subtract).then_inc(*n.made(lo_made))
        dve_split(dve, at, first["mla_out"] + MH - 1)
        residual(first["mla_out"] + MH - 1, 0, xn2)

        norm(1, 1, xn2, first["moe"])
        for b in range(NB):
            for i in range(2):
                dve.wait_ge(*n.next(t_full))
                dve.tensor_copy(h2n[:, b, i * TILE:(i + 1) * TILE], tb()[:, :]).then_inc(*n.made(t_drained))
        mask, logit, index, best, second = (route[:, i] for i in range(5))
        gap = route[:, 6]
        dve.wait_ge(*n.next(t_full))
        step(dve.tensor_copy(logit, tb()[:, 0:NB * NEXP].rearrange("p (b e) -> p b e", b=NB)), t_drained)
        for b in range(NB):
            step(dve.max(top8[:, b, :], logit[:, b, :]))
            step(dve.max_index(topi[:, b, :], top8[:, b, :], logit[:, b, :]))
        step(dve.tensor_copy(index, topi[:, :, :]))
        for b in range(NB):
            for i, dst in enumerate((best, second)):
                step(dve.tensor_scalar(dst[:, b, :], const("iota", 0, NEXP), index[:, b, i:i + 1], None, ALU.is_equal))
        step(dve.tensor_tensor(mask, best, second, ALU.add), mask_ready)
        step(dve.tensor_tensor(gap[:, :, 0:1], top8[:, :, 1:2], top8[:, :, 0:1], ALU.subtract), gap_ready)
        dve.memset(posm[:, :, NEXP:NEXP + 1], -BIG)
        dve.memset(gates8[:, :, NEXP:NEXP + 1], 0.0)
        step(dve.memset(y_moe[:, :, :], 0.0))
        dve.wait_ge(*n.next(exp_ready))
        step(dve.tensor_scalar(gap[:, :, 1:2], gap[:, :, 0:1], 1.0, None, ALU.add))
        step(dve.reciprocal(gap[:, :, 2:3], gap[:, :, 1:2]))
        step(dve.tensor_tensor(gap[:, :, 3:4], gap[:, :, 0:1], gap[:, :, 2:3], ALU.mult))
        for b in range(NB):
            step(dve.tensor_scalar(gates8[:, b, 0:NEXP], best[:, b, :], gap[:, b, 2:3], None, ALU.mult))
            step(dve.scalar_tensor_tensor(gates8[:, b, 0:NEXP], second[:, b, :], gap[:, b, 3:4], gates8[:, b, 0:NEXP],
                                          ALU.mult, ALU.add))
        dve.wait_ge(*n.next(t_full))
        t = tb()
        step(dve.scalar_tensor_tensor(posm[:, :, 0:NEXP], t[:, 0:NB * NEXP].rearrange("p (b e) -> p b e", b=NB), BIG,
                                      mask, ALU.add, ALU.mult))
        step(dve.tensor_scalar(posm[:, :, 0:NEXP], posm[:, :, 0:NEXP], -BIG, None, ALU.add))
        step(dve.tensor_reduce(small[:, 0:1], t[:, 2 * NEXP:3 * NEXP], AX.X, ALU.max), t_drained)
        step(dve.tensor_copy(flag[:, :], small[:, 0:1]), flag_ready)

        def places(base, e):
            slots = const("iota", 0, P) if base == 0 else const("iota", P, 2 * P)
            for b in range(NB):
                dve.tensor_scalar(place_m[:, b, :], slots, posm[:, b, e], None, ALU.is_equal)
                ins = dve.tensor_scalar(place_g[:, b, :], slots, posm[:, b, e], gates8[:, b, e], ALU.is_equal,
                                        ALU.mult)
            ins.then_inc(*n.made(placed))

        def split_into(hi, lo, a):
            dve.wait_ge(*n.next(t_full))
            dve.wait_ge(*n.next(hi_made))
            dve.tensor_tensor(lo[:, a:a + 4, :], tb()[:, :].rearrange("p (k t) -> p k t", k=4),
                              hi[:, a:a + 4, :].bitcast(F32), ALU.subtract).then_inc(*n.made(t_drained))

        def combine(i):
            dve.wait_ge(*n.next(t_full))
            y = y_moe[:, i // 2, i % 2 * TILE:(i % 2 + 1) * TILE]
            dve.tensor_tensor(y, tb()[:, :], y, ALU.add).then_inc(*n.made(t_drained))

        def experts(base):
            at = Place()
            at.base = base
            step(dve.memset(placeT[:, :], 0.0), zeroed)
            places(base, slice(0, 1))
            split_into(xeTh, xeTl, 0)
            split_into(xeTh, xeTl, 4)
            with dve.Fori(0, NEXP) as e:
                at.reg = e
                n.enter(e, MOE_STEPS)
                for m in range(MOE_TILES):
                    dve_split_moe(dve, at, 8 * m + 3 + AHEAD)
                    if m == 0:
                        combine(0)
                        combine(1)
                    else:
                        split_into(eTh, eTl, 4 * (m - 1))
                    if m in (1, 2):
                        combine(m + 1)
                    if m == 3:
                        dve.wait_ge(*n.next(t_full))
                        dve.tensor_copy(placeT[:, :], tb()[:, 0:SEQ]).then_inc(*n.made(t_drained))
                    dve_split_moe(dve, at, 8 * m + 7 + AHEAD)
                    dve.wait_ge(*n.next(gate_read))
                    dve.wait_ge(*used(at, 8 * m + 7))
                    dve.tensor_tensor(e_nat[:, m % 2, :], bank[2 + m % 2][:, :], esil[:, m % 2, :],
                                      ALU.mult).then_inc(*n.made(a_ready))
                w_out = 8 * MOE_TILES
                dve_split_moe(dve, at, w_out + T_LAST + AHEAD)
                split_into(eTh, eTl, 4 * (MOE_TILES - 1))
                places(base, bass.ds(e + 1, 1))
                dve_split_moe(dve, at, w_out + G_FIRST + AHEAD)
                split_into(xeTh, xeTl, 0)
                dve_split_moe(dve, at, w_out + G_SECOND + AHEAD)
                split_into(xeTh, xeTl, 4)
                dve_split_moe(dve, at, 2 * MOE_CHUNKS - 1)
            n.leave(NEXP)
            for i in range(4):
                combine(i)
            dve.wait_ge(*n.last())
        experts(0)
        dve.wait_ge(flag_ready, 1)
        with dve.If(dve.value_load(flag[0:1, 0:1]) > P):
            experts(NEXP)
        for b in range(NB):
            step(dve.tensor_tensor(y_moe[:, b, :], y_moe[:, b, :], gates[:, 1, :], ALU.mult))
            step(dve.tensor_tensor(xres[:, b, :], xres[:, b, :], y_moe[:, b, :], ALU.add), x_ready)

    @block.gpsimd
    def _(pool):
        n = Tally()

        def rstd(a, width, mean, dst, count):
            pool.tensor_scalar(small[:, mean:mean + width], small[:, a:a + width], 1.0 / count, EPS, ALU.mult,
                               ALU.add).then_inc(*n.made(pool_step))
            pool.wait_ge(*n.last())
            pool.tensor_tensor(small[:, dst:dst + width], small[:, mean:mean + width], const("mhalf", 0, width),
                               ALU.pow).then_inc(*n.made(rstd_ready))
        by_head = lambda v: v.rearrange("p (h d) -> p h d", h=HPG)
        spread = lambda v: v.unsqueeze(2).to_broadcast([P, HPG, HDIM])
        pool.wait_ge(consts_landed, 16)
        pool.wait_ge(*n.next(ssq_ready, NB))
        rstd(0, NB, 2, 4, D)
        pool.wait_ge(small_landed, 16 * 7)
        pool.wait_ge(*n.next(dt_ready, 3))
        pool.wait_ge(t_drained, XS_FILLS)
        for stepno in range(2 * GROUPS + 1):
            if stepno < 2 * GROUPS:
                v = stepno
                g, b = v // 2, v % 2
                if v >= 2:
                    pool.wait_ge(*n.next(yg_ready))
                src = by_head(xs[:, b, g * GW:(g + 1) * GW])
                h = slice(g * HPG, (g + 1) * HPG)
                pool.tensor_tensor(by_head(xskip[:, b, :]), src, spread(head_rows[:, 2, h]), ALU.mult)
                if b:
                    pool.tensor_tensor(by_head(xend[:, :]), by_head(xs[:, 0, g * GW:(g + 1) * GW]),
                                       spread(dts[:, 4, 0, h]), ALU.mult)
                pool.tensor_tensor(by_head(xdt[:, b, :]), src, spread(dts[:, 0, b, h]), ALU.mult).then_inc(
                    *n.made(xdt_ready))
            if stepno:
                v = stepno - 1
                pool.wait_ge(*n.next(ssq_ready))
                rstd(8 + v, 1, 24 + v, 40 + v, GW)
        for phase in range(2 * DEPTH - 1):
            pool.wait_ge(*n.next(ssq_ready, NB))
            rstd(0, NB, 2, 4, D)
            if phase == 1:
                pool.wait_ge(*n.next(ssq_ready))
                rstd(8, 4, 12, 16, RANK)

    block_cm.__exit__(None, None, None)


_INS = ["x", "c", "positions", "ada_w", "ada_b", "norm1_g", "norm2_g", "ssd_w_in", "ssd_conv_w", "ssd_conv_b",
        "ssd_dt_bias", "ssd_a_log", "ssd_d", "ssd_norm_g", "ssd_w_out", "mla_w_in", "mla_q_norm_g", "mla_kv_norm_g",
        "mla_w_uq", "mla_w_ukv", "mla_q_nope_g", "mla_q_rope_g", "mla_k_nope_g", "mla_k_rope_g", "mla_w_out",
        "ffn_w_in", "ffn_w_out", "router_w", "moe_w_in", "moe_w_out"]


def kernel(**inputs):
    import numpy as _np
    import concourse.bacc as _bacc
    from concourse import mybir as _mybir
    from concourse.bass_utils import run_bass_kernel_spmd as _run

    nc = _bacc.Bacc("TRN2", target_bir_lowering=False, num_devices=1)
    arrays, args = {}, []
    for name in _INS:
        a = _np.ascontiguousarray(inputs[name])
        arrays[f"in_{name}_dram"] = a
        args.append(nc.dram_tensor(f"in_{name}_dram", a.shape, _mybir.dt.from_np(a.dtype), kind="ExternalInput").ap())
    a = shape_constants()
    arrays["in_consts_dram"] = a
    args.append(nc.dram_tensor("in_consts_dram", a.shape, _mybir.dt.from_np(a.dtype), kind="ExternalInput").ap())
    args.append(nc.dram_tensor("out_0_dram", (1, SEQ, D), _mybir.dt.from_np(_np.dtype("float32")),
                               kind="ExternalOutput").ap())
    build(nc, *args)
    r = _run(nc, [arrays], core_ids=[0])
    return r.results[0]["out_0_dram"]
```
